# Optimizing a Trainium2 kernel written in Bass

```python
import jax, jax.numpy as jnp
from jax import lax
import numpy as np

D_MODEL = 1024
BATCH = 1
SEQ = 128
DEPTH = 2
DEC_BATCH = 1
DEC_SEQ = 128
PAST_LEN = 128

GRID_W = 64
N_EVEN = (DEPTH + 1) // 2
N_ODD = DEPTH // 2
HEADS_A = 4
KEY_A = 128
VAL_A = (D_MODEL // 2) // HEADS_A
HGRN_CHUNK = 16
HEAD_DIM_B = 128
HEADS_B = (D_MODEL // 2) // HEAD_DIM_B
KV_HEADS_B = HEADS_B // 2
Q_BLOCK = 128
ROPE_BASE = 10000.0
HEADS_C = 4
KEY_C = D_MODEL // HEADS_C
VAL_C = 2 * KEY_C
RET_CHUNK = 128
N_GROUPS = 4
EXPERTS_PER_GROUP = 8
N_EXPERTS = N_GROUPS * EXPERTS_PER_GROUP
TOP_K_INNER = 2
D_EXPERT = D_MODEL // 4
EPS = 1e-6

EVEN_SPLITS = (HEADS_A * KEY_A, HEADS_A * VAL_A, HEADS_A * KEY_A, HEADS_A * KEY_A, HEADS_A * VAL_A,
               HEADS_B * HEAD_DIM_B, KV_HEADS_B * HEAD_DIM_B, KV_HEADS_B * HEAD_DIM_B)
EVEN_MIX = HEADS_A * VAL_A + HEADS_B * HEAD_DIM_B
ODD_SPLITS = (HEADS_C * KEY_C, HEADS_C * KEY_C, HEADS_C * VAL_C, HEADS_C * VAL_C)
ODD_MIX = HEADS_C * VAL_C

kernel_name = 'hybrid_flow_backbone_step'

F32 = jnp.float32

def split_cols(p, sizes):
    return jnp.split(p, [int(s) for s in np.cumsum(sizes)[:-1]], axis=-1)

def rms_norm(x, g):
    xf = x.astype(F32)
    y = xf * lax.rsqrt(jnp.mean(xf * xf, axis=-1, keepdims=True) + EPS)
    return (y * g.astype(F32)).astype(x.dtype)

def head_layer_norm(x, g):
    xf = x.astype(F32)
    mu = jnp.mean(xf, axis=-1, keepdims=True)
    var = jnp.mean(jnp.square(xf - mu), axis=-1, keepdims=True)
    return (xf - mu) * lax.rsqrt(var + EPS) * g.astype(F32)

def ada_mod(cvec, w, b):
    m = jax.nn.silu(cvec.astype(F32)) @ w.astype(F32) + b.astype(F32)
    return tuple(jnp.split(m[:, None, :], 6, axis=-1))

def modulate(h, shift, scale):
    return (h.astype(F32) * (1.0 + scale) + shift).astype(h.dtype)

def flip(t):
    return jnp.flip(t, axis=1)

def axial_rope(x):
    b, s, h, dh = x.shape
    rows = s // GRID_W
    row = jnp.repeat(jnp.arange(rows), GRID_W).astype(F32)
    col = jnp.tile(jnp.arange(GRID_W), rows).astype(F32)
    half = dh // 2
    n_freq = half // 2
    inv = ROPE_BASE ** (-jnp.arange(n_freq, dtype=F32) / n_freq)
    ang = jnp.concatenate([row[:, None] * inv, col[:, None] * inv], axis=-1)[None, :, None, :]
    cos, sin = jnp.cos(ang), jnp.sin(ang)
    xf = x.astype(F32)
    x1, x2 = xf[..., :half], xf[..., half:]
    return jnp.concatenate([x1 * cos - x2 * sin, x2 * cos + x1 * sin], axis=-1).astype(x.dtype)

def gqa_blocked(q, k, v):
    b, s, h, d = q.shape
    kvh = k.shape[2]
    grp = h // kvh
    qb = jnp.moveaxis(q.astype(F32).reshape(b, s // Q_BLOCK, Q_BLOCK, kvh, grp, d), 1, 0)
    kf, vf = k.astype(F32), v.astype(F32)
    scale = d ** -0.5

    def one_block(qblk):
        p = jax.nn.softmax(jnp.einsum('bqkgd,btkd->bkgqt', qblk, kf) * scale, axis=-1)
        return jnp.einsum('bkgqt,btkd->bqkgd', p, vf)

    o = lax.map(one_block, qb)
    return jnp.moveaxis(o, 0, 1).reshape(b, s, h * d).astype(q.dtype)

def hgrn_gates(z, lb):
    z = z.astype(F32)
    logf = jnp.log(lb + (1.0 - lb) * jax.nn.sigmoid(z))
    key = (1.0 - lb) * jax.nn.sigmoid(-z)
    return logf, key

def hgrn2_chunked(q, k, v, logf, s0):
    b, t, h, kd = q.shape
    vd = v.shape[-1]
    L = HGRN_CHUNK
    n = t // L
    q, k, logf = (a.reshape(b, n, L, h, kd) for a in (q, k, logf))
    v = v.reshape(b, n, L, h, vd)
    cum = jnp.cumsum(logf, axis=2)
    causal = (jnp.arange(L)[:, None] >= jnp.arange(L)[None, :])[None, None, :, :, None, None]
    decay = jnp.exp(jnp.where(causal, cum[:, :, :, None] - cum[:, :, None, :], -jnp.inf))
    scores = jnp.einsum('bnthk,bnshk,bntshk->bnhts', q, k, decay)
    o = jnp.einsum('bnhts,bnshv->bnthv', scores, v)
    last = cum[:, :, -1]
    kv = jnp.einsum('bnshk,bnshv->bnhkv', k * jnp.exp(last[:, :, None] - cum), v)

    def step(state, inp):
        dec, kvc = inp
        return dec[..., None] * state + kvc, state

    s_fin, s_start = lax.scan(step, s0, (jnp.moveaxis(jnp.exp(last), 1, 0), jnp.moveaxis(kv, 1, 0)))
    o = o + jnp.einsum('bnthk,bnhkv->bnthv', q * jnp.exp(cum), jnp.moveaxis(s_start, 0, 1))
    return o.reshape(b, t, h, vd), s_fin

def retention_chunked(q, k, v, log_gamma, s0):
    b, t, h, kd = q.shape
    vd = v.shape[-1]
    L = RET_CHUNK
    n = t // L
    q = q.reshape(b, n, L, h, kd)
    k = k.reshape(b, n, L, h, kd)
    v = v.reshape(b, n, L, h, vd)
    j = jnp.arange(L, dtype=F32)
    rel = (j[:, None] - j[None, :])[None]
    dmat = jnp.exp(jnp.where(rel >= 0, rel * log_gamma[:, None, None], -jnp.inf))
    o = jnp.einsum('bnhts,bnshv->bnthv', jnp.einsum('bnthk,bnshk->bnhts', q, k) * dmat, v)
    k_dec = k * jnp.exp((L - 1.0 - j)[:, None] * log_gamma)[:, :, None]
    kv = jnp.einsum('bnshk,bnshv->bnhkv', k_dec, v)
    chunk_dec = jnp.exp(L * log_gamma)[:, None, None]

    def step(state, kvc):
        return chunk_dec * state + kvc, state

    s_fin, s_start = lax.scan(step, s0, jnp.moveaxis(kv, 1, 0))
    q_dec = q * jnp.exp((j + 1.0)[:, None] * log_gamma)[:, :, None]
    o = o + jnp.einsum('bnthk,bnhkv->bnthv', q_dec, jnp.moveaxis(s_start, 0, 1))
    return o.reshape(b, t, h, vd), s_fin

def even_mixer(h, w_in, w_out, lb, hgrn_g, qn_g, kn_g, ctx=None):
    b, s, _ = h.shape
    qa, ia, zf, zb, ga, qb, kb, vb = split_cols(h @ w_in, EVEN_SPLITS)
    qa = jax.nn.silu(qa.astype(F32)).reshape(b, s, HEADS_A, KEY_A) * KEY_A ** -0.5
    ia = ia.astype(F32).reshape(b, s, HEADS_A, VAL_A)
    lb = lb.reshape(2, HEADS_A, KEY_A)
    logf_f, key_f = hgrn_gates(zf.reshape(b, s, HEADS_A, KEY_A), lb[0])
    logf_b, key_b = hgrn_gates(zb.reshape(b, s, HEADS_A, KEY_A), lb[1])
    if ctx is None:
        s0 = jnp.zeros((b, 2, HEADS_A, KEY_A, VAL_A), F32)
    else:
        s0 = ctx[2].astype(F32)
    o_f, s_f = hgrn2_chunked(qa, key_f, ia, logf_f, s0[:, 0])
    o_b, s_b = hgrn2_chunked(flip(qa), flip(key_b), flip(ia), flip(logf_b), s0[:, 1])
    oa = rms_norm(o_f + flip(o_b), hgrn_g).reshape(b, s, HEADS_A * VAL_A) * jax.nn.silu(ga.astype(F32))
    qb = rms_norm(qb.reshape(b, s, HEADS_B, HEAD_DIM_B), qn_g)
    kb = rms_norm(kb.reshape(b, s, KV_HEADS_B, HEAD_DIM_B), kn_g)
    vb = vb.reshape(b, s, KV_HEADS_B, HEAD_DIM_B)
    if ctx is None:
        ob = gqa_blocked(qb, kb, vb)
    else:
        k_all = jnp.concatenate([ctx[0].astype(kb.dtype), axial_rope(kb)], axis=1)
        v_all = jnp.concatenate([ctx[1].astype(vb.dtype), vb], axis=1)
        ob = gqa_blocked(axial_rope(qb), k_all, v_all)
    out = jnp.concatenate([oa.astype(h.dtype), ob.astype(h.dtype)], axis=-1) @ w_out
    if ctx is None:
        return out, (kb, vb, jnp.stack([s_f, s_b], axis=1).astype(h.dtype))
    return out, None

def odd_mixer(h, w_in, w_out, decay_logit, gn_g, ctx=None):
    b, s, _ = h.shape
    q, k, v, g = split_cols(h @ w_in, ODD_SPLITS)
    q = q.reshape(b, s, HEADS_C, KEY_C)
    k = k.reshape(b, s, HEADS_C, KEY_C) * KEY_C ** -0.5
    if ctx is not None:
        q, k = axial_rope(q), axial_rope(k)
    q, k = q.astype(F32), k.astype(F32)
    v = v.astype(F32).reshape(b, s, HEADS_C, VAL_C)
    log_gamma = jax.nn.log_sigmoid(decay_logit.astype(F32))
    if ctx is None:
        s0 = jnp.zeros((b, 2, HEADS_C, KEY_C, VAL_C), F32)
    else:
        s0 = ctx.astype(F32)
    o_f, s_f = retention_chunked(q, k, v, log_gamma[0], s0[:, 0])
    o_b, s_b = retention_chunked(flip(q), flip(k), flip(v), log_gamma[1], s0[:, 1])
    y = head_layer_norm(o_f + flip(o_b), gn_g).reshape(b, s, ODD_MIX)
    out = (jax.nn.silu(g.astype(F32)) * y).astype(h.dtype) @ w_out
    if ctx is None:
        return out, jnp.stack([s_f, s_b], axis=1).astype(h.dtype)
    return out, None

def hier_moe(h, w_group, b_group, w_expert, b_expert, w_gate, w_up, w_down):
    b, s, d = h.shape
    x = h.reshape(b * s, d)
    xf = x.astype(F32)
    g_prob = jax.nn.softmax(xf @ w_group.astype(F32) + b_group.astype(F32), axis=-1)
    p_grp, g_idx = lax.top_k(g_prob, 1)
    e_logit = (xf @ w_expert.astype(F32) + b_expert.astype(F32)).reshape(-1, N_GROUPS, EXPERTS_PER_GROUP)
    e_logit = jnp.einsum('tge,tg->te', e_logit, jax.nn.one_hot(g_idx[:, 0], N_GROUPS, dtype=F32))
    e_w, e_idx = lax.top_k(jax.nn.softmax(e_logit, axis=-1), TOP_K_INNER)
    e_w = e_w / jnp.sum(e_w, axis=-1, keepdims=True) * p_grp
    combine = jnp.sum(jax.nn.one_hot(g_idx * EXPERTS_PER_GROUP + e_idx, N_EXPERTS, dtype=F32)
                      * e_w[..., None], axis=1)
    act = jax.nn.silu(jnp.einsum('td,edf->tef', x, w_gate)) * jnp.einsum('td,edf->tef', x, w_up)
    act = act * combine[..., None].astype(act.dtype)
    y = jnp.einsum('tef,efd->td', act, w_down)
    return y.reshape(b, s, d).astype(h.dtype)

def setup_inputs(seed: int = 0) -> dict:
    key = jax.random.key(seed)
    ks = iter(jax.random.split(key, 32))

    def nrm(shape, scale):
        return jax.random.normal(next(ks), shape, F32) * scale

    D = D_MODEL
    decay_base = jnp.log(2.0 ** (5.0 + jnp.arange(HEADS_C, dtype=F32)) - 1.0)
    return {
        'x_prompt': nrm((BATCH, SEQ, D), 1.0),
        'x_sample': nrm((DEC_BATCH, DEC_SEQ, D), 1.0),
        'cache_attn_k': nrm((DEC_BATCH, N_EVEN, PAST_LEN, KV_HEADS_B, HEAD_DIM_B), 1.0),
        'cache_attn_v': nrm((DEC_BATCH, N_EVEN, PAST_LEN, KV_HEADS_B, HEAD_DIM_B), 1.0),
        'state_hgrn': nrm((DEC_BATCH, N_EVEN, 2, HEADS_A, KEY_A, VAL_A), 0.5),
        'state_ret': nrm((DEC_BATCH, N_ODD, 2, HEADS_C, KEY_C, VAL_C), 0.5),
        'c': nrm((DEC_BATCH, D), 1.0),
        'c_ctx': nrm((D,), 1.0),
        'mod_w': nrm((DEPTH, D, 6 * D), 0.5 * D ** -0.5),
        'mod_b': nrm((DEPTH, 6 * D), 0.02),
        'norm1_g': 1.0 + nrm((DEPTH, D), 0.05),
        'norm2_g': 1.0 + nrm((DEPTH, D), 0.05),
        'even_w_in': nrm((N_EVEN, D, sum(EVEN_SPLITS)), D ** -0.5),
        'even_w_out': nrm((N_EVEN, EVEN_MIX, D), EVEN_MIX ** -0.5),
        'hgrn_lb_logits': nrm((DEPTH + 1, 2, HEADS_A * KEY_A), 0.5),
        'hgrn_norm_g': 1.0 + nrm((N_EVEN, HEADS_A, VAL_A), 0.05),
        'attn_qn_g': 1.0 + nrm((N_EVEN, HEAD_DIM_B), 0.05),
        'attn_kn_g': 1.0 + nrm((N_EVEN, HEAD_DIM_B), 0.05),
        'odd_w_in': nrm((N_ODD, D, sum(ODD_SPLITS)), D ** -0.5),
        'odd_w_out': nrm((N_ODD, ODD_MIX, D), ODD_MIX ** -0.5),
        'ret_decay_logit': decay_base[None, None, :] + nrm((N_ODD, 2, HEADS_C), 0.1),
        'ret_gn_g': 1.0 + nrm((N_ODD, HEADS_C, VAL_C), 0.05),
        'moe_w_group': nrm((DEPTH, D, N_GROUPS), D ** -0.5),
        'moe_b_group': nrm((DEPTH, N_GROUPS), 0.01),
        'moe_w_expert': nrm((DEPTH, D, N_EXPERTS), D ** -0.5),
        'moe_b_expert': nrm((DEPTH, N_EXPERTS), 0.01),
        'moe_w_gate': nrm((DEPTH, N_EXPERTS, D, D_EXPERT), D ** -0.5),
        'moe_w_up': nrm((DEPTH, N_EXPERTS, D, D_EXPERT), D ** -0.5),
        'moe_w_down': nrm((DEPTH, N_EXPERTS, D_EXPERT, D), D_EXPERT ** -0.5),
        'final_norm_g': 1.0 + nrm((D,), 0.05),
    }

def reference(x_prompt, x_sample, cache_attn_k, cache_attn_v, state_hgrn, state_ret, c, c_ctx,
              mod_w, mod_b, norm1_g, norm2_g, even_w_in, even_w_out, hgrn_lb_logits, hgrn_norm_g,
              attn_qn_g, attn_kn_g, odd_w_in, odd_w_out, ret_decay_logit, ret_gn_g,
              moe_w_group, moe_b_group, moe_w_expert, moe_b_expert, moe_w_gate, moe_w_up, moe_w_down,
              final_norm_g):
    lower_bounds = jnp.cumsum(jax.nn.softmax(hgrn_lb_logits.astype(F32), axis=0), axis=0)
    xc, xs = x_prompt, x_sample
    new_k, new_v, new_sh, new_sr = [], [], [], []
    for l in range(DEPTH):
        mc = ada_mod(c_ctx[None], mod_w[l], mod_b[l])
        ms = ada_mod(c, mod_w[l], mod_b[l])
        hc = modulate(rms_norm(xc, norm1_g[l]), mc[0], mc[1])
        hs = modulate(rms_norm(xs, norm1_g[l]), ms[0], ms[1])
        if l % 2 == 0:
            e = l // 2
            args = (even_w_in[e], even_w_out[e], lower_bounds[l], hgrn_norm_g[e], attn_qn_g[e], attn_kn_g[e])
            oc, (kc, vc, sc) = even_mixer(hc, *args)
            os_, _ = even_mixer(hs, *args, ctx=(cache_attn_k[:, e], cache_attn_v[:, e], state_hgrn[:, e]))
            new_k.append(kc)
            new_v.append(vc)
            new_sh.append(sc)
        else:
            o = l // 2
            args = (odd_w_in[o], odd_w_out[o], ret_decay_logit[o], ret_gn_g[o])
            oc, sc = odd_mixer(hc, *args)
            os_, _ = odd_mixer(hs, *args, ctx=state_ret[:, o])
            new_sr.append(sc)
        xc = xc + (mc[2] * oc.astype(F32)).astype(xc.dtype)
        xs = xs + (ms[2] * os_.astype(F32)).astype(xs.dtype)
        moe_args = (moe_w_group[l], moe_b_group[l], moe_w_expert[l], moe_b_expert[l],
                    moe_w_gate[l], moe_w_up[l], moe_w_down[l])
        hc = modulate(rms_norm(xc, norm2_g[l]), mc[3], mc[4])
        hs = modulate(rms_norm(xs, norm2_g[l]), ms[3], ms[4])
        xc = xc + (mc[5] * hier_moe(hc, *moe_args).astype(F32)).astype(xc.dtype)
        xs = xs + (ms[5] * hier_moe(hs, *moe_args).astype(F32)).astype(xs.dtype)
    y_prompt = rms_norm(xc, final_norm_g)
    y_sample = rms_norm(xs, final_norm_g)
    new_attn_k = jnp.stack(new_k, axis=1)
    new_attn_v = jnp.stack(new_v, axis=1)
    new_state_hgrn = jnp.stack(new_sh, axis=1)
    new_state_ret = jnp.stack(new_sr, axis=1)
    return (y_prompt, y_sample, new_attn_k, new_attn_v, new_state_hgrn, new_state_ret)


_drawn_inputs = setup_inputs


def setup_inputs(seed=0):
    import zlib

    import numpy as np

    out = dict(_drawn_inputs(seed))
    spreads = {}
    factors = {'cache_attn_k': 3.681,
     'state_hgrn': 8.0,
     'hgrn_norm_g': 5.767,
     'attn_qn_g': 8.0,
     'ret_gn_g': 4.241,
     'moe_b_group': 13.932,
     'moe_b_expert': 8.0}
    for name, (base, spread) in spreads.items():
        noise = np.random.default_rng([zlib.crc32(name.encode()), seed]).standard_normal(out[name].shape)
        drawn = base * np.exp(spread * noise) if base else spread * noise
        out[name] = __import__('jax').numpy.asarray(drawn.astype(out[name].dtype))
    for name, factor in factors.items():
        out[name] = (out[name] * factor).astype(out[name].dtype)
    return out
```

```python
from contextlib import ExitStack

import concourse.bass as bass
from concourse import mybir
from concourse.alu_op_type import AluOpType as ALU

ACT = mybir.ActivationFunctionType
AX = mybir.AxisListType.X
F32 = mybir.dt.float32
I32 = mybir.dt.int32
SIGMOID, SILU, EXP, LN, SQRT, SQUARE, COPY = (
    ACT.Sigmoid, ACT.Silu, ACT.Exp, ACT.Ln, ACT.Sqrt, ACT.Square, ACT.Copy)

P = 128
S = 2
D = 1024
KT = D // P
EPS = 1e-6
BANK = 512
SUB = 32
NSUB = P // SUB
HA = 4
HB = 4
KVH = 2
HC = 4
VC = 512
NG, EG = 4, 8
NE = NG * EG
FE = 256
CAP = 64
NPAIR = NE // 2
ROUNDS = S * P // CAP
RING = 6
SLOT = 4096
MB = 6
BIG = 1.0e30

CONST_PARTS = [
    ("ident", P), ("cums", 2 * 3 * P), ("relp", P), ("relm", P), ("ge", P), ("le", P),
    ("powers", 4), ("rowf", P), ("rowb", P), ("cosb", 64), ("sinb", 64), ("cosc", P), ("sinc", P), ("upper", P),
    ("ones", P), ("slots", CAP), ("selb", 2 * S * 2 * P), ("tie4", NG), ("tie8", EG)]
CONST_AT = {}
_n = 0
for _name, _w in CONST_PARTS:
    CONST_AT[_name] = (_n, _n + _w)
    _n += _w
NCONST = _n

QA, IA_, ZF, ZB, GA, QB, KVB = range(7)
EVEN_ORDER = [ZF, ZB, QA, IA_, QB, KVB, GA]


def weight_stream():
    items = [("mod", 0, b, q) for b in (0, 1) for q in (0, 1)]
    items += [("even_in", c) for c in EVEN_ORDER]
    items += [("mod", l, b, q) for l, b in MOD_LATE for q in (0, 1)]
    items += [("even_out", q) for q in range(2)]
    items += [("moe", 0, p, m) for p in range(NPAIR) for m in range(3)]
    items += [("odd_in", c) for c in range(8)]
    items += [("state", d) for d in range(2)]
    items += [("odd_in", c) for c in range(8, 12)]
    items += [("odd_out", q) for q in range(4)]
    items += [("moe", 1, p, m) for p in range(NPAIR) for m in range(3)]
    return items


MOD_LATE = [(0, b) for b in range(2, MB)] + [(1, b) for b in range(MB)]
STREAM = weight_stream()
AT = {item: n for n, item in enumerate(STREAM)}


def backbone(nc, A, O):
    ctx = ExitStack()
    with ctx:
        def sb(name, shape, dt=F32):
            return ctx.enter_context(nc.sbuf_tensor(name, shape, dt))

        def sem(name):
            return ctx.enter_context(nc.semaphore(name))

        ring = sb("ring", [P, RING, SLOT])
        const = sb("const", [P, NCONST])
        X = sb("X", [P, S, D])
        H = sb("H", [P, S, KT, P])
        HT = sb("HT", [P, 8, S * P])
        modrow = sb("modrow", [P, MB, BANK])
        gain = sb("gain", [P, D])
        scratch = sb("scratch", [P, 11264])
        cvec = sb("cvec", [P, S, KT])
        cpad = sb("cpad", [P, KT, 36])
        lbcol = sb("lbcol", [P, 3, 8])
        lbtmp = sb("lbtmp", [P, 3, 8])
        lb = sb("lb", [P, 2, 8])
        small = sb("small", [P, 160])
        csig = small[:, 120:136].rearrange("p (s k) -> p s k", s=S)
        PS = ctx.enter_context(nc.psum_tensor("PS", [P, 8, BANK], F32))

        def cst(name):
            a, b = CONST_AT[name]
            return const[:, a:b]

        ident = cst("ident")
        cums_c = cst("cums").rearrange("p (d n) -> p d n", d=2)
        zero = cums_c[0:1, 0, 2 * P:3 * P]
        selb_c = cst("selb").rearrange("p (l s h t) -> p l s h t", l=2, s=S, h=2)
        powers_c = cst("powers")

        def carve(at, *shape):
            n = 1
            for x in shape:
                n *= x
            v = scratch[:, at:at + n]
            if len(shape) == 2:
                v = v.rearrange("p (a b) -> p a b", a=shape[0])
            if len(shape) == 3:
                v = v.rearrange("p (a b c) -> p a b c", a=shape[0], b=shape[1])
            return v, at + n

        lbrow = scratch[0:24, 11264 - P:11264]
        normed, _at = carve(0, S, D)
        squares, _at = carve(_at, S, D)
        gated, _ = carve(0, S, D)
        sumsq, rstd = small[:, 0:2], small[:, 2:4]

        QT, _at = carve(0, HA, S * P)
        IV, _at = carve(_at, S, 512)
        KEYT, _at = carve(_at, 2, HA, S * P)
        GS, _at = carve(_at, S, 512)
        QKV, _at = carve(_at, S, 8, P)
        LFT, _at = carve(_at, HA, P)
        K2, _at = carve(_at, HA, P)
        ST, _at = carve(_at, 4, 512)
        S0A, _at = carve(_at, 2, 512)
        _evend = _at
        LF = H[:, :, :, :].rearrange("p s k c -> p (s k c)").rearrange("p (d h t) -> p d h t", d=2, h=HA)
        SG = ST.rearrange("p a n -> p (a n)")[:, 0:1024].rearrange("p (h t) -> p h t", h=HA)
        assert _evend <= 11264
        E = sb("E", [P, 4 * BANK])
        E1 = E[:, 0:512].rearrange("p (h k) -> p h k", h=HA)
        E1N = E[:, 512:1024].rearrange("p (h k) -> p h k", h=HA)
        E23 = E[:, 1024:2048].rearrange("p (h k) -> p h k", h=HA)
        DEC = small[:, 8:24].rearrange("p (h n) -> p h n", h=HA)
        GNA = LFT.rearrange("p h k -> p (h k)")
        QNG = sb("QNG", [P, 2, P])
        CKV = sb("CKV", [P, 2, 2 * P])
        ssA, rsA = small[:, 24:32], small[:, 32:40]
        AT_, _at = carve(0, 8, P)
        PR, _at = carve(1024, HB, 2 * P)
        PRT, _at = carve(2048, 8, P)
        SQ, _at = carve(2048, S, 6, P)
        SQf = scratch[:, 2048:2048 + 4 * 384].rearrange("p (a n c) -> p a n c", a=4, n=6)
        ssB, rsB = small[:, 40:52], small[:, 52:64]
        mxB, nbB, smB, riB = small[:, 64:68], small[:, 68:72], small[:, 72:76], small[:, 76:80]

        QKc, _at = carve(0, S, 2048)
        VY, _at = carve(_at, S, 2048)
        DM, _at = carve(_at, HC, P)
        TT, _at = carve(_at, 4, P)
        QD, _at = carve(_at, 4, P)
        PC, _at = carve(_at, P)
        KD, _at = carve(_at, 2, 2 * P)
        LGP, _at = carve(_at, 2, P)
        bnC, _at = carve(_at, S, HC, 6)
        mvC, _at = carve(_at, S * HC, 2)
        assert _at <= 11264, _at
        MIXC = QKc.rearrange("p s n -> p (s n)").rearrange("p (k t) -> p k t", k=16)
        GNC = H[:, :, :, :].rearrange("p s k c -> p (s k c)")
        SF = E[:, :].rearrange("p (a v) -> p a v", a=4)
        LG = small[:, 80:88]
        KDC = small[:, 88:104]
        sdC, rsC = small[:, 104:112], small[:, 112:120]

        XG, _at = carve(0, 2, KT, P)
        SEL, _at = carve(_at, 2, S, P)
        WSEL, _at = carve(_at, 2, S, P)
        WSELT, _at = carve(_at, 2, S, P)
        SILB, _at = carve(_at, FE)
        ACTB, _at = carve(_at, FE)
        ACTT, _at = carve(_at, 2, P)
        YG, _at = carve(_at, 2, BANK)
        LGT, _at = carve(_at, S, NG + NE)
        G4, _at = carve(_at, 3, S * NG)
        PRD, _at = carve(_at, S * NG, EG)
        E8, _at = carve(_at, 8, S * EG)
        MASK, _at = carve(_at, S, NE)
        CW, _at = carve(_at, S, NE + 2)
        POS, _at = carve(_at, S, NE + 2)
        assert _at <= 11264
        s1 = small[:, 120:150]
        RW = sb("RW", [P, KT, NG + NE])
        CNT = sb("CNT", [P, 2], I32)
        rbias = sb("rbias", [1, 2, NG + NE])

        landed = [sem(f"landed{i}") for i in range(RING)]
        used = sem("used")
        params_in = sem("params_in")
        x_in = sem("x_in")
        pad_clear = sem("pad_clear")
        bias_in = sem("bias_in")
        cast_done = sem("cast_done")
        c_sig = sem("c_sig")
        c_ready = sem("c_ready")
        mod_ready = sem("mod_ready")
        lb_t = sem("lb_t")
        lb_sub = sem("lb_sub")
        lb_exp = sem("lb_exp")
        lb_ready = sem("lb_ready")
        x_ready = sem("x_ready")
        gain_in = sem("gain_in")
        gain_used = sem("gain_used")
        sq_ready = sem("sq_ready")
        std_ready = sem("std_ready")
        bc_done = sem("bc_done")
        h_ready = sem("h_ready")
        ht_done = sem("ht_done")
        ht_ready = sem("ht_ready")
        v_step = sem("v_step")
        a_step = sem("a_step")
        gate_done = sem("gate_done")
        gate_ready = sem("gate_ready")
        branch_done = sem("branch_done")
        in_free_a = sem("in_free_a")
        in_free_v = sem("in_free_v")
        sg_ready = sem("sg_ready")
        f_ready = sem("f_ready")
        lf_ready = sem("lf_ready")
        key_ready = sem("key_ready")
        gs_act = sem("gs_act")
        gs_ready = sem("gs_ready")
        lft_done = sem("lft_done")
        lft_ready = sem("lft_ready")
        cums_done = sem("cums_done")
        exps_ready = sem("exps_ready")
        qk_ready = sem("qk_ready")
        scores_done = sem("scores_done")
        k2_done = sem("k2_done")
        pt_ready = sem("pt_ready")
        k2_ready = sem("k2_ready")
        kv_done = sem("kv_done")
        states_ready = sem("states_ready")
        group_done = sem("group_done")
        state_out = sem("state_out")
        oa_std = sem("oa_std")
        oa_ready = sem("oa_ready")
        oat_done = sem("oat_done")
        mix_ready = sem("mix_ready")
        b_ss = sem("b_ss")
        b_std = sem("b_std")
        b_ready = sem("b_ready")
        bt_done = sem("bt_done")
        bt_ready = sem("bt_ready")
        bs_done = sem("bs_done")
        b_max = sem("b_max")
        b_exp = sem("b_exp")
        b_prob = sem("b_prob")
        bp_done = sem("bp_done")
        bp_ready = sem("bp_ready")
        bo_done = sem("bo_done")
        out_sem = sem("out_sem")
        c_free_a = sem("c_free_a")
        c_free_v = sem("c_free_v")
        c_lg = sem("c_lg")
        c_dm = sem("c_dm")
        c_rope = sem("c_rope")
        c_pow = sem("c_pow")
        ct_done = sem("ct_done")
        ct_ready = sem("ct_ready")
        cd_ready = sem("cd_ready")
        cs_done = sem("cs_done")
        cp_ready = sem("cp_ready")
        kd_ready = sem("kd_ready")
        co_done = sem("co_done")
        cstate_done = sem("cstate_done")
        sf_ready = sem("sf_ready")
        sf_out = [sem(f"sf_out{i}") for i in range(4)]
        c_std = sem("c_std")
        c_y = sem("c_y")
        g_act = sem("g_act")
        g_ready = sem("g_ready")
        cm_done = sem("cm_done")
        cm_ready = sem("cm_ready")
        gn_in = sem("gn_in")
        rw_in = sem("rw_in")
        logit_done = sem("logit_done")
        r_gexp_in = sem("r_gexp_in")
        r_gexp = sem("r_gexp")
        r_exp_in = sem("r_exp_in")
        r_exp = sem("r_exp")
        mask_ready = sem("mask_ready")
        prefix_done = sem("prefix_done")
        count_ready = sem("count_ready")
        sel_ready = sem("sel_ready")
        wsel_ready = sem("wsel_ready")
        gather0_done = sem("gather0_done")
        gather1_done = sem("gather1_done")
        turn_done = sem("turn_done")
        wselt_ready = sem("wselt_ready")
        actt_ready = sem("actt_ready")
        xg0_ready = sem("xg0_ready")
        xg1_ready = sem("xg1_ready")
        silu_ready = sem("silu_ready")
        act_ready = sem("act_ready")
        down0_done = sem("down0_done")
        yg0_ready = sem("yg0_ready")
        yg1_ready = sem("yg1_ready")
        OV = [{n: sem(f"ov{l}_{n}") for n in
               ("sel", "gath", "xg", "sil", "act", "turn", "actt", "yg", "scat", "in0", "in1", "in2",
                "used", "shift")} for l in range(2)]

        block = ctx.enter_context(nc.Block())

        def slot(item):
            return AT[item] % RING

        def arrived(eng, item):
            n = AT[item]
            eng.wait_ge(landed[n % RING], 16 * (n // RING + 1))

        def bcast(ap, shape):
            return ap.broadcast_to(shape)

        class Steps:

            def __init__(self, eng, s):
                self.eng, self.sem, self.n = eng, s, 0

            def link(self, ins):
                self.mark(ins)
                self.wait()

            def mark(self, ins):
                ins.then_inc(self.sem, 1)
                self.n += 1

            def wait(self):
                self.eng.wait_ge(self.sem, self.n)

        @block.sync
        def _(sp):
            def source(item):
                kind = item[0]
                if kind == "mod":
                    _, l, b, q = item
                    v = A["mod_w"][l].rearrange("(p k) n -> p k n", k=KT)
                    return v[:, 4 * q:4 * q + 4, D * b:D * b + D]
                if kind == "even_in":
                    v = A["even_w_in"][0].rearrange("(p k) n -> p k n", k=KT)
                    return v[:, :, 512 * item[1]:512 * item[1] + 512]
                if kind == "odd_in":
                    v = A["odd_w_in"][0].rearrange("(p k) n -> p k n", k=KT)
                    return v[:, :, 512 * item[1]:512 * item[1] + 512]
                if kind == "state":
                    return A["state_ret"][0, 0, item[1]].rearrange("h (j p) v -> p (h j) v", p=P)
                w = A["even_w_out"] if kind == "even_out" else A["odd_w_out"]
                return w[0].rearrange("(k p) n -> p k n", p=P)[:, 4 * item[1]:4 * item[1] + 4, :]

            def load(n):
                src = source(STREAM[n])
                dst = ring[:, n % RING, :].rearrange("p (a b) -> p a b", b=src.shape[2])
                if n >= RING:
                    sp.wait_ge(used, n - RING + 1)
                sp.dma_start(dst, src).then_inc(landed[n % RING], 16)

            def expert_source(l, m, p):
                if m < 2:
                    w = A["moe_w_gate" if m == 0 else "moe_w_up"][l].rearrange("e (p k) f -> p e (k f)", p=P)
                    return w[:, bass.ds(p * 2, 2), :]
                w = A["moe_w_down"][l].rearrange("e (j p) n -> p (e j) n", p=P)
                return w[:, bass.ds(p * 4, 4), :]

            n = 0
            while n < len(STREAM):
                if STREAM[n][0] != "moe":
                    load(n)
                    n += 1
                    continue
                l, first = STREAM[n][1], n
                with sp.Fori(0, NPAIR // 2) as i:
                    for u in range(2):
                        for m in range(3):
                            k = first + 3 * u + m
                            sp.wait_ge(used, i * RING + (k - RING + 1))
                            src = expert_source(l, m, i * 2 + u)
                            dst = ring[:, k % RING, :].rearrange("p (a b) -> p a b", b=src.shape[2])
                            sp.dma_start(dst, src).then_inc(landed[k % RING], 16)
                n += 3 * NPAIR
                sp.wait_ge(count_ready, l + 1)
                most = sp.value_load(CNT[0:1, 0:1], min_val=0, max_val=S * P)
                with sp.If(most > CAP):
                    ov = OV[l]
                    sp.wait_ge(used, n)
                    with sp.Fori(0, ROUNDS - 1) as r:
                        with sp.Fori(0, NPAIR) as p:
                            for m in range(3):
                                sp.wait_ge(ov["used"], (r * NPAIR + p) * 3)
                                src = expert_source(l, m, p)
                                dst = ring[:, m, :].rearrange("p (a b) -> p a b", b=src.shape[2])
                                sp.dma_start(dst, src).then_inc(ov[f"in{m}"], 16)
                    sp.wait_ge(ov["used"], (ROUNDS - 1) * NPAIR * 3)

        @block.gpsimd
        def _(pool):
            def router_weights(l):
                pool.dma_start(RW[:, :, 0:NG], A["moe_w_group"][l].rearrange("(p k) g -> p k g", k=KT))\
                    .then_inc(rw_in, 16)
                pool.dma_start(RW[:, :, NG:], A["moe_w_expert"][l].rearrange("(p k) g -> p k g", k=KT))\
                    .then_inc(rw_in, 16)

            pool.dma_start(const[:, :], A["consts"]).then_inc(params_in, 16)
            pool.dma_start(cvec[:, 0, :], A["c_ctx"].rearrange("(p k) -> p k", k=KT)).then_inc(params_in, 16)
            pool.dma_start(cvec[:, 1, :], A["c"][0].rearrange("(p k) -> p k", k=KT)).then_inc(params_in, 16)
            pool.dma_start(lbrow[:, :], A["hgrn_lb_logits"].rearrange("a b (h k) -> (a b h) k", k=P))\
                .then_inc(params_in, 16)
            pool.dma_start(X[:, 0, :], A["x_prompt"][0]).then_inc(x_in, 16)
            pool.dma_start(X[:, 1, :], A["x_sample"][0]).then_inc(x_in, 16)
            pool.dma_start(gain[:, :], A["norm1_g"][0].partition_broadcast(P)).then_inc(gain_in, 16)
            pool.wait_ge(pad_clear, 3)
            for l in range(2):
                mb = A["mod_b"][l].rearrange("(b h n) -> h b n", h=2, n=BANK)
                for half in range(2):
                    for s in range(S):
                        r = 32 * half + 2 * l + s
                        pool.dma_start(modrow[r:r + 1, :, :], mb[half:half + 1]).then_inc(bias_in, 16)
            router_weights(0)
            pool.dma_start(QNG[:, 0, :], A["attn_qn_g"][0].partition_broadcast(P)).then_inc(cast_done, 16)
            pool.dma_start(QNG[:, 1, :], A["attn_kn_g"][0].partition_broadcast(P)).then_inc(cast_done, 16)
            pool.dma_start(CKV[:, 0, :], A["cache_attn_k"][0, 0].rearrange("t h d -> t (h d)")).then_inc(cast_done, 16)
            pool.dma_start(CKV[:, 1, :], A["cache_attn_v"][0, 0].rearrange("t h d -> t (h d)")).then_inc(cast_done, 16)
            for l in range(2):
                pool.dma_start(rbias[:, l, 0:NG], A["moe_b_group"][l:l + 1]).then_inc(cast_done, 16)
                pool.dma_start(rbias[:, l, NG:], A["moe_b_expert"][l:l + 1]).then_inc(cast_done, 16)
            pool.dma_start(small[:, 80:88], A["ret_decay_logit"][0].rearrange("a b -> (a b)").partition_broadcast(P))\
                .then_inc(cast_done, 16)

            def next_gain(n, src):
                pool.wait_ge(gain_used, n)
                pool.dma_start(gain[:, :], src.partition_broadcast(P)).then_inc(gain_in, 16)

            pool.wait_ge(h_ready, 4)
            pool.dma_start(GNA, A["hgrn_norm_g"][0].rearrange("h v -> (h v)").partition_broadcast(P))\
                .then_inc(cast_done, 16)
            for d in range(2):
                pool.dma_start(S0A[:, d, :].rearrange("p (h v) -> p h v", h=HA),
                               A["state_hgrn"][0, 0, d].rearrange("h k v -> k h v")).then_inc(cast_done, 16)
            next_gain(1, A["norm2_g"][0])
            for d in range(2):
                pool.wait_ge(states_ready, d + 1)
                pool.dma_start(O["new_state_hgrn"][0, 0, d].rearrange("h k v -> k h v"),
                               ST[:, 3, :].rearrange("p (h v) -> p h v", h=HA)).then_inc(state_out, 16)
            pool.wait_ge(b_ready, 1)
            pool.dma_start(O["new_attn_k"][0, 0].rearrange("t h d -> t (h d)"),
                           QKV[:, 0, 4:6, :].rearrange("p a b -> p (a b)")).then_inc(out_sem, 16)
            pool.dma_start(O["new_attn_v"][0, 0].rearrange("t h d -> t (h d)"),
                           QKV[:, 0, 6:8, :].rearrange("p a b -> p (a b)")).then_inc(out_sem, 16)
            pool.wait_ge(out_sem, 32)
            next_gain(2, A["norm1_g"][1])
            pool.wait_ge(logit_done, 1)
            router_weights(1)
            pool.wait_ge(ht_ready, 12)
            pool.dma_start(GNC, A["ret_gn_g"][0].rearrange("h v -> (h v)").partition_broadcast(P)).then_inc(gn_in, 16)
            next_gain(3, A["norm2_g"][1])
            for n in range(2 * HC * 2):
                pool.wait_ge(sf_ready, n + 1)
                h, d, j = n // 4, (n // 2) % 2, n % 2
                pool.dma_start(O["new_state_ret"][0, 0, d, h, P * j:P * j + P, :], SF[:, n % 4, :])\
                    .then_inc(sf_out[n % 4], 16)
            for n in range(4):
                pool.wait_ge(sf_out[n], 16 * HC)
            next_gain(4, A["final_norm_g"])
            pool.wait_ge(h_ready, 18)
            pool.dma_start(O["y_prompt"][0], normed[:, 0, :]).then_inc(out_sem, 16)
            pool.dma_start(O["y_sample"][0], normed[:, 1, :]).then_inc(out_sem, 16)
            pool.wait_ge(out_sem, 64)
            pool.wait_ge(state_out, 32)

        @block.tensor
        def _(pe):
            def matmul(out, lhsT, rhs, start, stop, **kw):
                return nc.tensor.matmul(out, lhsT, rhs, start=start, stop=stop, skip_group_check=True, **kw)

            def mod_block(l, b, n, bank):
                if n >= 1:
                    pe.wait_ge(mod_ready, n)
                for q in range(2):
                    item = ("mod", l, b, q)
                    arrived(pe, item)
                    w = ring[:, slot(item), :].rearrange("p (k n) -> p k n", k=4)
                    for k in range(4):
                        for half in range(2):
                            g = 2 * (k % 2) + half
                            mm = matmul(PS[32 * g:32 * g + 32, bank, :], cpad[:, 4 * q + k, 2 - 2 * l:34 - 2 * l],
                                        w[:, k, BANK * half:BANK * half + BANK],
                                        start=(q == 0 and k < 2), stop=(q == 1 and k >= 2))
                    mm.then_inc(used, 1)

            def broadcast(bank, l, b, s):
                for half in range(2):
                    mm = matmul(PS[:, bank + half, :], selb_c[:, l, s, half, :], modrow[:, b, :], True, True)
                return mm

            def norm(n):
                l, w = n // 2, n % 2
                pe.wait_ge(mod_ready, 2 + len(MOD_LATE) if n else 2)
                if n:
                    pe.wait_ge(x_ready, 2 * n)
                for s in range(S):
                    broadcast(2 * s, l, 3 * w + 1, s)
                    broadcast(4 + 2 * s, l, 3 * w, s).then_inc(bc_done, 1)
                for s in range(S):
                    pe.wait_ge(h_ready, 4 * n + 2 * (s + 1))
                    for k in range(KT):
                        mm = nc.tensor.transpose(PS[:, 2 * s + k // 4, P * (k % 4):P * (k % 4) + P],
                                                 H[:, s, k, :], ident)
                    mm.then_inc(ht_done, 1)

            def gates(n):
                l, w = n // 2, n % 2
                for s in range(S):
                    mm = broadcast(4 + 2 * s, l, 3 * w + 2, s)
                mm.then_inc(gate_done, 1)

            pe.wait_ge(params_in, 64)
            nc.tensor.transpose(PS[:, 1, 0:24], lbrow[:, :], ident[0:24, 0:24]).then_inc(lb_t, 1)
            pe.wait_ge(c_ready, 1)
            pe.wait_ge(pad_clear, 3)
            mod_block(0, 0, 0, 0)
            mod_block(0, 1, 1, 0)
            pe.wait_ge(lb_ready, 1)
            norm(0)

            pe.wait_ge(ht_ready, 4)
            for i, c in enumerate(EVEN_ORDER):
                item = ("even_in", c)
                bank = 2 * (i % 4)
                if i in (4, 5):
                    pe.wait_ge(in_free_a, i - 3)
                if i == 6:
                    pe.wait_ge(in_free_v, 1)
                arrived(pe, item)
                w = ring[:, slot(item), :].rearrange("p (k n) -> p k n", k=KT)
                if c in (QA, ZF, ZB):
                    for h in range(HA):
                        for k in range(KT):
                            mm = matmul(PS[:, bank + h // 2, 256 * (h % 2):256 * (h % 2) + 256],
                                        w[:, k, P * h:P * h + P], HT[:, k, :], k == 0, k == KT - 1)
                else:
                    for s in range(S):
                        for k in range(KT):
                            mm = matmul(PS[:, bank + s, :], HT[:, k, P * s:P * s + P], w[:, k, :],
                                        k == 0, k == KT - 1)
                mm.then_inc(used, 1)

            late = list(MOD_LATE)

            def late_mod(k):
                for _ in range(k):
                    l, b = late.pop(0)
                    mod_block(l, b, 2 + len(MOD_LATE) - len(late) - 1, 5)

            pe.wait_ge(in_free_a, 5)
            pe.wait_ge(in_free_v, 4)
            pe.wait_ge(gs_act, 1)
            for g in range(4):
                s, d = g // 2, g % 2
                pe.wait_ge(lf_ready, d + 1)
                if g:
                    pe.wait_ge(pt_ready, g)
                for h in range(HA):
                    mm = nc.tensor.transpose(PS[:, 4, P * h:P * h + P], LF[:, d, h, P * s:P * s + P], ident)
                mm.then_inc(lft_done, 1)
                if g:
                    pe.wait_ge(k2_ready, g)
                late_mod(2)
                pe.wait_ge(lft_ready, g + 1)
                if g:
                    pe.wait_ge(states_ready, g)
                for h in range(HA):
                    mm = matmul(PS[:, h, 0:3 * P], LFT[:, h, :], cums_c[:, d, :], True, True)
                mm.then_inc(cums_done, 1)
                pe.wait_ge(qk_ready, 4 * (g + 1))
                for h in range(HA):
                    mm = matmul(PS[:, 4, P * h:P * h + P], E1N[:, h, :], E1[:, h, :], True, True)
                mm.then_inc(scores_done, 1)
                pe.wait_ge(mod_ready, 2 + len(MOD_LATE) - len(late))
                for h in range(HA):
                    mm = nc.tensor.transpose(PS[:, 5, P * h:P * h + P], E23[:, h, P:2 * P], ident)
                mm.then_inc(k2_done, 1)
                pe.wait_ge(k2_ready, g + 1)
                for n in range(NSUB):
                    for h in range(HA):
                        mm = matmul(PS[:, n, P * h:P * h + P], K2[SUB * n:SUB * n + SUB, h, :],
                                    IV[SUB * n:SUB * n + SUB, s, P * h:P * h + P], True, True)
                mm.then_inc(kv_done, 1)
                pe.wait_ge(pt_ready, g + 1)
                for h in range(HA):
                    matmul(PS[:, 6 + s, P * h:P * h + P], LFT[:, h, :], IV[:, s, P * h:P * h + P],
                           d == 0 and h == 0, False)
                pe.wait_ge(states_ready, g + 1)
                order = list(range(NSUB)) if d == 0 else list(range(NSUB))[::-1]
                for i, n in enumerate(order):
                    if i == 0 and s == 0:
                        continue
                    for h in range(HA):
                        start_state = S0A[:, d, P * h:P * h + P] if i == 0 else ST[:, i - 1, P * h:P * h + P]
                        mm = matmul(PS[SUB * n:SUB * n + SUB, 6 + s, P * h:P * h + P],
                                    E23[:, h, SUB * n:SUB * n + SUB], start_state, False, True)
                mm.then_inc(group_done, 1)
            for s in range(S):
                pe.wait_ge(oa_ready, s + 1)
                if s:
                    pe.wait_ge(mix_ready, 1)
                for h in range(HA):
                    mm = nc.tensor.transpose(PS[:, 4, P * h:P * h + P], GS[:, s, P * h:P * h + P], ident)
                mm.then_inc(oat_done, 1)

            pe.wait_ge(mix_ready, 2)
            for s in range(S):
                nk = 1 + s
                pe.wait_ge(b_ready, s + 1)
                if s:
                    pe.wait_ge(bp_ready, 1)
                for j in range(6):
                    mm = nc.tensor.transpose(PS[:, j // 4, P * (j % 4):P * (j % 4) + P], QKV[:, s, j, :], ident)
                if s:
                    for j in range(KVH):
                        mm = nc.tensor.transpose(PS[:, 1, P * (2 + j):P * (3 + j)], CKV[:, 0, P * j:P * j + P], ident)
                mm.then_inc(bt_done, 1)
                late_mod(1)
                pe.wait_ge(bt_ready, s + 1)
                if s:
                    pe.wait_ge(mix_ready, 3)
                for h in range(HB):
                    for t in range(nk):
                        at = (h * nk + t) * P
                        mm = matmul(PS[:, 2 + at // BANK, at % BANK:at % BANK + P], AT_[:, h, :],
                                    AT_[:, 4 + 2 * t + h // 2, :], True, True)
                mm.then_inc(bs_done, 1)
                pe.wait_ge(b_prob, s + 1)
                for j in range(HB * nk):
                    mm = nc.tensor.transpose(PS[:, j // 4, P * (j % 4):P * (j % 4) + P],
                                             PR[:, j // nk, P * (j % nk):P * (j % nk) + P], ident)
                mm.then_inc(bp_done, 1)
                pe.wait_ge(bp_ready, s + 1)
                for h in range(HB):
                    for t in range(nk):
                        kv = h // 2
                        v = QKV[:, s, 6 + kv, :] if t == 0 else CKV[:, 1, P * kv:P * kv + P]
                        mm = matmul(PS[:, 2, P * h:P * h + P], v, PRT[:, h * nk + t, :], t == 0, t == nk - 1)
                mm.then_inc(bo_done, 1)
            assert not late

            def project_out(kind, chunks, src, n):
                for q in range(chunks):
                    item = (kind, q)
                    arrived(pe, item)
                    w = ring[:, slot(item), :].rearrange("p (k n) -> p k n", k=4)
                    for k in range(4):
                        kk = 4 * q + k
                        for s in range(S):
                            for half in range(2):
                                mm = matmul(PS[:, 2 * s + half, :], src[:, kk, P * s:P * s + P],
                                            w[:, k, BANK * half:BANK * half + BANK],
                                            kk == 0, kk == 4 * chunks - 1)
                    mm.then_inc(used, 1)
                gates(n)

            pe.wait_ge(mix_ready, 4)
            pe.wait_ge(mod_ready, 2 + len(MOD_LATE))
            project_out("even_out", 2, HT, 0)

            def moe(l):
                base = AT[("moe", l, 0, 0)]
                ov = OV[l]
                pe.wait_ge(ht_ready, 4 * (2 * l + 2))
                pe.wait_ge(rw_in, 32 * (l + 1))
                pe.wait_ge(cast_done, 16 * 12)
                for s in range(S):
                    for k in range(KT):
                        matmul(PS[:, 4, 64 * s:64 * s + NG + NE], HT[:, k, P * s:P * s + P], RW[:, k, :], k == 0, False)
                    mm = matmul(PS[:, 4, 64 * s:64 * s + NG + NE], cst("ones")[0:1, :], rbias[:, l, :], False, True)
                mm.then_inc(logit_done, 1)
                for b in range(4):
                    matmul(PS[:, b, :], zero, const[0:1, 0:BANK], True, False)
                pe.wait_ge(mask_ready, l + 1)
                matmul(PS[:, 5, 0:NE], cst("upper"), MASK[:, 0, :], True, True)
                matmul(PS[:, 5, 64:64 + NE], cst("ones"), MASK[:, 0, :], True, False)
                matmul(PS[:, 5, 64:64 + NE], cst("upper"), MASK[:, 1, :], False, True)
                matmul(PS[:, 5, 128:128 + NE], cst("ones"), MASK[:, 0, :], True, False)
                matmul(PS[:, 5, 128:128 + NE], cst("ones"), MASK[:, 1, :], False, True).then_inc(prefix_done, 1)

                def gather(half, par):
                    for k in range(4):
                        for s in range(S):
                            mm = matmul(PS[:, 4 + half, P * k:P * k + P], H[:, s, 4 * half + k, :],
                                        SEL[:, par, s, :], s == 0, s == S - 1)
                    return mm

                def turn_select(par):
                    for s in range(S):
                        mm = nc.tensor.transpose(PS[:, 7, 256 + P * s:256 + P * s + P], WSEL[:, par, s, :], ident)
                    return mm

                def turn_act():
                    for j in range(2):
                        mm = nc.tensor.transpose(PS[:, 7, P * j:P * j + P], ACTB[:, P * j:P * j + P], ident)
                    return mm

                def gate_or_up(m, slot_, par):
                    w = ring[:, slot_, :].rearrange("p (e k f) -> p e k f", e=2, k=KT)
                    for k in range(KT):
                        for e in range(2):
                            mm = matmul(PS[CAP * e:CAP * e + CAP, 6, FE * m:FE * m + FE],
                                        XG[:, par, k, CAP * e:CAP * e + CAP], w[:, e, k, :], k == 0, k == KT - 1)
                    return mm

                def down(half, slot_):
                    w = ring[:, slot_, :].rearrange("p (e j n) -> p e j n", e=2, j=2)
                    for j in range(2):
                        for e in range(2):
                            mm = matmul(PS[CAP * e:CAP * e + CAP, 4 + half, :], ACTT[:, j, CAP * e:CAP * e + CAP],
                                        w[:, e, j, BANK * half:BANK * half + BANK], j == 0, j == 1)
                    return mm

                def scatter(par):
                    for s in range(S):
                        for half in range(2):
                            mm = matmul(PS[:, 2 * s + half, :], WSELT[:, par, s, :], YG[:, half, :], False, False)
                    return mm

                def pair(p, par, first=False, last=False):
                    t = p + 16 * l
                    lap = (base + 3 * par) // RING
                    sl = [(base + 3 * par + m) % RING for m in range(3)]
                    lv = [16 * ((base + 3 * par + m) // RING + 1) for m in range(3)]
                    p2 = (p - par) * 8
                    pe.wait_ge(xg0_ready, t + 1)
                    pe.wait_ge(xg1_ready, t + 1)
                    if not (first and l == 0):
                        pe.wait_ge(act_ready, t)
                    pe.wait_ge(landed[sl[0]], p2 + lv[0])
                    gate_or_up(0, sl[0], par).then_inc(used, 1)
                    if not first:
                        pe.wait_ge(yg0_ready, t)
                        pe.wait_ge(yg1_ready, t)
                        pe.wait_ge(wselt_ready, t)
                        scatter(1 - par)
                    pe.wait_ge(landed[sl[1]], p2 + lv[1])
                    gate_or_up(1, sl[1], par).then_inc(used, 1)
                    if not last:
                        pe.wait_ge(sel_ready, p * 2 + (34 * l + 4))
                        gather(0, 1 - par).then_inc(gather0_done, 1)
                        pe.wait_ge(wsel_ready, p * 2 + (34 * l + 4))
                        pe.wait_ge(wselt_ready, t + 1)
                        turn_select(1 - par)
                    pe.wait_ge(act_ready, t + 1)
                    turn_act().then_inc(turn_done, 1)
                    if not last:
                        gather(1, 1 - par).then_inc(gather1_done, 1)
                        pe.wait_ge(xg0_ready, t + 2)
                    pe.wait_ge(actt_ready, t + 1)
                    pe.wait_ge(landed[sl[2]], p2 + lv[2])
                    down(0, sl[2]).then_inc(down0_done, 1)
                    if not last:
                        pe.wait_ge(xg1_ready, t + 2)
                    down(1, sl[2]).then_inc(used, 1)

                pe.wait_ge(sel_ready, 34 * l + 2)
                gather(0, 0).then_inc(gather0_done, 1)
                gather(1, 0).then_inc(gather1_done, 1)
                pe.wait_ge(wsel_ready, 34 * l + 2)
                turn_select(0).then_inc(turn_done, 1)
                pair(0, 0, first=True)
                with pe.Fori(0, NPAIR // 2 - 1) as i:
                    pair(i * 2 + 1, 1)
                    pair(i * 2 + 2, 0)
                pair(NPAIR - 1, 1, last=True)
                pe.wait_ge(yg0_ready, 16 * l + NPAIR)
                pe.wait_ge(yg1_ready, 16 * l + NPAIR)
                pe.wait_ge(wselt_ready, 16 * l + NPAIR)
                scatter(1)

                pe.wait_ge(count_ready, l + 1)
                most = pe.value_load(CNT[0:1, 0:1], min_val=0, max_val=S * P)
                with pe.If(most > CAP):
                    with pe.Fori(0, ROUNDS - 1) as r:
                        with pe.Fori(0, NPAIR) as p:
                            t = r * NPAIR + p
                            pe.wait_ge(ov["sel"], t * 4 + 4)
                            pe.wait_ge(ov["yg"], t * 2)
                            gather(0, 0)
                            gather(1, 0)
                            turn_select(0).then_inc(ov["gath"], 1)
                            pe.wait_ge(ov["xg"], t * 3 + 3)
                            pe.wait_ge(ov["in0"], t * 16 + 16)
                            gate_or_up(0, 0, 0).then_inc(ov["used"], 1)
                            pe.wait_ge(ov["in1"], t * 16 + 16)
                            gate_or_up(1, 1, 0).then_inc(ov["used"], 1)
                            pe.wait_ge(ov["act"], t + 1)
                            turn_act().then_inc(ov["turn"], 1)
                            pe.wait_ge(ov["actt"], t + 1)
                            pe.wait_ge(ov["in2"], t * 16 + 16)
                            down(0, 2)
                            down(1, 2).then_inc(ov["used"], 1)
                            pe.wait_ge(ov["yg"], t * 2 + 2)
                            scatter(0).then_inc(ov["scat"], 1)
                matmul(PS[:, 3, :], zero, const[0:1, 0:BANK], False, True).then_inc(branch_done, 1)
                gates(2 * l + 1)

            norm(1)
            moe(0)
            norm(2)

            pe.wait_ge(ht_ready, 12)

            def odd_chunk(c, i, consumed=1):
                item = ("odd_in", c)
                bank = 2 * (i % 4)
                if i >= 4:
                    pe.wait_ge(c_free_a, i - 3)
                    pe.wait_ge(c_free_v, i - 3)
                arrived(pe, item)
                w = ring[:, slot(item), :].rearrange("p (k n) -> p k n", k=KT)
                for s in range(S):
                    for k in range(KT):
                        mm = matmul(PS[:, bank + s, :], HT[:, k, P * s:P * s + P], w[:, k, :], k == 0, k == KT - 1)
                mm.then_inc(used, consumed)

            for c in range(8):
                odd_chunk(c, c)
            pe.wait_ge(c_free_a, 8)
            pe.wait_ge(c_free_v, 8)
            pe.wait_ge(c_dm, HC)
            arrived(pe, ("state", 0))
            arrived(pe, ("state", 1))
            for s in range(S):
                for h in range(HC):
                    u = HC * s + h
                    if s:
                        pe.wait_ge(c_rope, 1)
                    if u:
                        pe.wait_ge(ct_ready, u)
                    for j in range(4):
                        src = QKc[:, s, 1024 * (j // 2) + 256 * h + P * (j % 2):1024 * (j // 2) + 256 * h + P * (j % 2) + P]
                        mm = nc.tensor.transpose(PS[:, 0, P * j:P * j + P], src, ident)
                    mm.then_inc(ct_done, 1)
                    pe.wait_ge(ct_ready, u + 1)
                    for j in range(2):
                        mm = matmul(PS[:, 1, 0:P], TT[:, 2 + j, :], TT[:, j, :], j == 0, j == 1)
                    mm.then_inc(cs_done, 1)
                    if s == 0:
                        pe.wait_ge(kd_ready, 2 * (h + 1))
                        for d in range(2):
                            for j in range(2):
                                n = 4 * h + 2 * d + j
                                if n >= 4:
                                    pe.wait_ge(sf_ready, n - 3)
                                matmul(PS[:, 4 + n % 4, :], KD[:, d, P * j:P * j + P],
                                       VY[:, 0, VC * h:VC * h + VC], True, True).then_inc(cstate_done, 1)
                    pe.wait_ge(cp_ready, u + 1)
                    if u:
                        pe.wait_ge(c_y, u)
                    mm = matmul(PS[:, 2, :], PC, VY[:, s, VC * h:VC * h + VC], True, s == 0)
                    if s:
                        pe.wait_ge(cd_ready, h + 1)
                        for d in range(2):
                            st = ring[:, slot(("state", d)), :].rearrange("p (h j v) -> p h j v", h=HC, j=2)
                            for j in range(2):
                                mm = matmul(PS[:, 2, :], QD[:, 2 * d + j, :], st[:, h, j, :], False, d == 1 and j == 1)
                    mm.then_inc(co_done, 1)
            pe.wait_ge(c_y, 2 * HC)
            pe.wait_ge(sf_ready, 16)
            for i in range(4):
                odd_chunk(8 + i, 8 + i, consumed=1 if i else 3)
            for s in range(S):
                for q in range(4):
                    u = 4 * s + q
                    pe.wait_ge(g_ready, 2 * (q + 1))
                    if u >= 2:
                        pe.wait_ge(cm_ready, u - 1)
                    for j in range(4):
                        mm = nc.tensor.transpose(PS[:, 2 * 0 + u % 2, P * j:P * j + P],
                                                 VY[:, s, BANK * q + P * j:BANK * q + P * j + P], ident)
                    mm.then_inc(cm_done, 1)
            pe.wait_ge(cm_ready, 8)
            project_out("odd_out", 4, MIXC, 2)
            norm(3)
            moe(1)

        @block.scalar
        def _(act):
            st = Steps(act, a_step)
            A_ = nc.scalar.activation

            def norm(n):
                act.wait_ge(x_ready, 2 * n) if n else act.wait_ge(x_in, 32)
                for s in range(S):
                    A_(squares[:, s, :], X[:, s, :], SQUARE, accum_out=sumsq[:, s:s + 1]).then_inc(sq_ready, 1)
                act.wait_ge(sq_ready, 2 * n + 2)
                A_(sumsq, sumsq, SQRT, scale=1.0 / D, bias=EPS_COL).then_inc(std_ready, 1)

            def evac_ht(n):
                for s in range(S):
                    act.wait_ge(ht_done, 2 * n + s + 1)
                    A_(HT[:, 0:4, P * s:P * s + P], PS[:, 2 * s, :].rearrange("p (k t) -> p k t", k=4), COPY)\
                        .then_inc(ht_ready, 1)

            def residual(n):
                act.wait_ge(gate_done, n + 1)
                for s in range(S):
                    A_(gated[:, s, :], PS[:, 4 + 2 * s:6 + 2 * s, :].rearrange("p b n -> p (b n)"), COPY)\
                        .then_inc(gate_ready, 1)

            EPS_COL = small[:, 150:151]
            act.wait_ge(params_in, 64)
            act.wait_ge(pad_clear, 3)
            A_(csig, cvec[:, :, :], SIGMOID).then_inc(c_sig, 1)
            act.wait_ge(lb_sub, 1)
            A_(lbtmp[:, :, :], lbtmp[:, :, :], EXP).then_inc(lb_exp, 1)
            norm(0)
            evac_ht(0)

            for i, c in enumerate(EVEN_ORDER):
                bank = 2 * (i % 4)
                flat = PS[:, bank:bank + 2, :].rearrange("p b n -> p (b n)")
                byhead = flat.rearrange("p (h t) -> p h t", h=HA)
                act.wait_ge(used, AT[("even_in", c)] + 1)
                if c in (ZF, ZB):
                    d = 0 if c == ZF else 1
                    A_(LF[:, d, :, :], byhead, SIGMOID).then_inc(f_ready, 1)
                    A_(KEYT[:, d, :, :], byhead, SIGMOID, scale=-1.0).then_inc(in_free_a, 1)
                elif c == QA:
                    A_(SG[:, :, :], byhead, SIGMOID).then_inc(sg_ready, 1)
                elif c == IA_:
                    A_(IV[:, 0, :], PS[:, bank, :], COPY).then_inc(in_free_a, 1)
                elif c == QB:
                    A_(QKV[:, 0, 0:4, :], PS[:, bank, :].rearrange("p (a b) -> p a b", a=4), COPY).then_inc(in_free_a, 1)
                elif c == KVB:
                    A_(QKV[:, 0, 4:8, :], PS[:, bank, :].rearrange("p (a b) -> p a b", a=4), COPY).then_inc(in_free_a, 1)
                else:
                    A_(GS[:, :, :].rearrange("p s n -> p (s n)"), flat, SILU).then_inc(gs_act, 1)
                if c == QA:
                    for d in range(2):
                        act.wait_ge(key_ready, 2 * d + 1)
                        A_(LF[:, d, :, :], LF[:, d, :, :], LN).then_inc(lf_ready, 1)
            for g in range(4):
                act.wait_ge(cums_done, g + 1)
                if g:
                    act.wait_ge(group_done, g)
                A_(E1[:, :, :], PS[:, 0:4, 0:P], EXP).then_inc(exps_ready, 1)
                A_(E1N[:, :, :], PS[:, 0:4, 0:P], EXP, scale=-1.0).then_inc(exps_ready, 1)
                A_(E23[:, :, :], PS[:, 0:4, P:3 * P], EXP).then_inc(exps_ready, 1)
                act.wait_ge(k2_done, g + 1)
                A_(K2[:, :, :], PS[:, 5, :].rearrange("p (h k) -> p h k", h=HA), COPY).then_inc(k2_ready, 1)
            act.wait_ge(group_done, 4)
            for s in range(S):
                for h in range(HA):
                    st.link(A_(E1[:, 0, :], PS[:, 6 + s, P * h:P * h + P], SQUARE,
                               accum_out=ssA[:, HA * s + h:HA * s + h + 1]))
            st.wait()
            A_(ssA, ssA, SQRT, scale=1.0 / P, bias=EPS_COL).then_inc(oa_std, 1)
            for s in range(S):
                act.wait_ge(oat_done, s + 1)
                A_(HT[:, 0:4, P * s:P * s + P], PS[:, 4, :].rearrange("p (k t) -> p k t", k=4), COPY)\
                    .then_inc(mix_ready, 1)
            act.wait_ge(b_ss, 2)
            A_(ssB, ssB, SQRT, scale=1.0 / P, bias=EPS_COL).then_inc(b_std, 1)
            for s in range(S):
                nk = 1 + s
                act.wait_ge(bt_done, s + 1)
                A_(AT_[:, 0:6 + 2 * s, :].rearrange("p a b -> p (a b)"),
                   PS[:, 0:2, :].rearrange("p b n -> p (b n)")[:, 0:P * (6 + 2 * s)], COPY).then_inc(bt_ready, 1)
                act.wait_ge(b_max, s + 1)
                for h in range(HB):
                    src = PS[:, 2:4, :].rearrange("p b n -> p (b n)")[:, P * nk * h:P * nk * (h + 1)]
                    A_(PR[:, h, 0:P * nk], src, EXP, scale=float(P) ** -0.5, bias=nbB[:, h:h + 1],
                       accum_out=smB[:, h:h + 1]).then_inc(b_exp, 1)
                act.wait_ge(bp_done, s + 1)
                A_(PRT[:, 0:4 * nk, :].rearrange("p a b -> p (a b)"),
                   PS[:, 0:2, :].rearrange("p b n -> p (b n)")[:, 0:BANK * nk], COPY).then_inc(bp_ready, 1)
                act.wait_ge(bo_done, s + 1)
                A_(HT[:, 4:8, P * s:P * s + P], PS[:, 2, :].rearrange("p (k t) -> p k t", k=4), COPY)\
                    .then_inc(mix_ready, 1)
            residual(0)

            def moe(l):
                ov = OV[l]
                act.wait_ge(r_gexp_in, l + 1)
                A_(G4[:, 1, :], G4[:, 1, :], EXP).then_inc(r_gexp, 1)
                act.wait_ge(r_exp_in, l + 1)
                A_(s1[:, 8:10], s1[:, 8:10], EXP).then_inc(r_exp, 1)

                def xg_half(half, par):
                    return A_(XG[:, par, 4 * half:4 * half + 4, :].rearrange("p k t -> p (k t)"), PS[:, 4 + half, :], COPY)

                def wselt(par):
                    return A_(WSELT[:, par, :, :].rearrange("p s t -> p (s t)"), PS[:, 7, 256:512], COPY)

                def pair(p, par, last=False):
                    t = p + 16 * l
                    act.wait_ge(used, p * 3 + (AT[("moe", l, 0, 0)] + 2))
                    A_(SILB, PS[:, 6, 0:FE], SILU).then_inc(silu_ready, 1)
                    if not last:
                        act.wait_ge(gather0_done, t + 2)
                        xg_half(0, 1 - par).then_inc(xg0_ready, 1)
                    act.wait_ge(turn_done, p + (17 * l + 2))
                    A_(ACTT[:, :, :].rearrange("p j t -> p (j t)"), PS[:, 7, 0:256], COPY).then_inc(actt_ready, 1)
                    if not last:
                        wselt(1 - par).then_inc(wselt_ready, 1)
                    act.wait_ge(used, p * 3 + (AT[("moe", l, 0, 0)] + 3))
                    A_(YG[:, 1, :], PS[:, 5, :], COPY).then_inc(yg1_ready, 1)

                act.wait_ge(gather0_done, 16 * l + 1)
                xg_half(0, 0).then_inc(xg0_ready, 1)
                act.wait_ge(turn_done, 17 * l + 1)
                wselt(0).then_inc(wselt_ready, 1)
                pair(0, 0)
                with act.Fori(0, NPAIR // 2 - 1) as i:
                    pair(i * 2 + 1, 1)
                    pair(i * 2 + 2, 0)
                pair(NPAIR - 1, 1, last=True)
                act.wait_ge(count_ready, l + 1)
                most = act.value_load(CNT[0:1, 0:1], min_val=0, max_val=S * P)
                with act.If(most > CAP):
                    with act.Fori(0, ROUNDS - 1) as r:
                        with act.Fori(0, NPAIR) as p:
                            t = r * NPAIR + p
                            act.wait_ge(ov["gath"], t + 1)
                            xg_half(0, 0).then_inc(ov["xg"], 1)
                            xg_half(1, 0).then_inc(ov["xg"], 1)
                            wselt(0).then_inc(ov["xg"], 1)
                            act.wait_ge(ov["used"], t * 3 + 2)
                            A_(SILB, PS[:, 6, 0:FE], SILU).then_inc(ov["sil"], 1)
                            act.wait_ge(ov["turn"], t + 1)
                            A_(ACTT[:, :, :].rearrange("p j t -> p (j t)"), PS[:, 7, 0:256], COPY)\
                                .then_inc(ov["actt"], 1)
                            act.wait_ge(ov["used"], t * 3 + 3)
                            A_(YG[:, 0, :], PS[:, 4, :], COPY).then_inc(ov["yg"], 1)
                            A_(YG[:, 1, :], PS[:, 5, :], COPY).then_inc(ov["yg"], 1)
                residual(2 * l + 1)

            norm(1)
            evac_ht(1)
            moe(0)
            norm(2)
            evac_ht(2)
            act.wait_ge(cast_done, 16 * 12)
            st.link(A_(LG, LG, SIGMOID))
            A_(LG, LG, LN).then_inc(c_lg, 1)

            def evac_odd(c, i):
                bank = 2 * (i % 4)
                act.wait_ge(used, AT[("odd_in", c)] + 1)
                dst = QKc[:, 0, 512 * c:512 * c + 512] if c < 4 else VY[:, 0, 512 * (c - 4):512 * (c - 4) + 512]
                A_(dst, PS[:, bank, :], COPY).then_inc(c_free_a, 1)

            for c in range(8):
                evac_odd(c, c)
            act.wait_ge(c_lg, 1)
            for d in range(2):
                for h in range(HC):
                    j = HC * d + h
                    st.mark(A_(KDC[:, j:j + 1], powers_c[:, 2 + d:3 + d], EXP, scale=LG[:, j:j + 1]))
            for h in range(HC):
                if h:
                    act.wait_ge(c_dm, h)
                A_(LGP[:, 0, :], cst("relp"), EXP, scale=LG[:, h:h + 1]).then_inc(c_pow, 1)
                A_(LGP[:, 1, :], cst("relm"), EXP, scale=LG[:, HC + h:HC + h + 1]).then_inc(c_pow, 1)
            act.wait_ge(c_dm, HC)
            for s in range(S):
                for h in range(HC):
                    u = HC * s + h
                    act.wait_ge(ct_done, u + 1)
                    if u:
                        act.wait_ge(co_done, u)
                    A_(TT[:, :, :].rearrange("p a b -> p (a b)"), PS[:, 0, :], COPY).then_inc(ct_ready, 1)
                    if s:
                        if h:
                            act.wait_ge(cd_ready, h)
                        A_(LGP[:, 0, :], cst("rowf"), EXP, scale=LG[:, h:h + 1]).then_inc(c_pow, 1)
                        A_(LGP[:, 1, :], cst("rowb"), EXP, scale=LG[:, HC + h:HC + h + 1]).then_inc(c_pow, 1)
                    else:
                        for j in range(4):
                            n = 4 * h + j
                            act.wait_ge(cstate_done, n + 1)
                            if n >= 4:
                                act.wait_ge(sf_out[n % 4], 16 * (n // 4))
                            A_(SF[:, n % 4, :], PS[:, 4 + n % 4, :], COPY).then_inc(sf_ready, 1)
                    act.wait_ge(c_std, 2 * u + 1)
                    A_(sdC[:, u:u + 1], mvC[:, u, 1:2], SQRT, bias=EPS_COL).then_inc(c_std, 1)
            act.wait_ge(sf_out[0], 16 * HC)
            act.wait_ge(sf_out[1], 16 * HC)
            for i in range(4):
                act.wait_ge(used, AT[("odd_in", 8 + i)] + 1)
                bank = 2 * ((8 + i) % 4)
                if i:
                    act.wait_ge(g_ready, 2 * i)
                A_(SF[:, 0:2, :].rearrange("p a b -> p (a b)"),
                   PS[:, bank:bank + 2, :].rearrange("p b n -> p (b n)"), SILU).then_inc(g_act, 1)
            for u in range(8):
                s, q = u // 4, u % 4
                if u % 2 == 0:
                    act.wait_ge(cm_done, u + 1)
                    A_(MIXC[:, 4 * q:4 * q + 4, P * s:P * s + P], PS[:, 0, :].rearrange("p (k t) -> p k t", k=4), COPY)\
                        .then_inc(cm_ready, 1)
                else:
                    act.wait_ge(cm_done, u + 1)
                    A_(MIXC[:, 4 * q:4 * q + 4, P * s:P * s + P], PS[:, 1, :].rearrange("p (k t) -> p k t", k=4), COPY)\
                        .then_inc(cm_ready, 1)
            residual(2)
            norm(3)
            evac_ht(3)
            moe(1)
            norm(4)

        @block.vector
        def _(dve):
            V = nc.vector
            st = Steps(dve, v_step)

            def mod_rows(l, b, n, bank):
                dve.wait_ge(used, AT[("mod", l, b, 1)] + 1)
                V.tensor_tensor(modrow[:, b, :], PS[:, bank, :], modrow[:, b, :], ALU.add).then_inc(mod_ready, 1)

            def norm(n, final=False):
                dve.wait_ge(std_ready, n + 1)
                st.link(V.reciprocal(rstd, sumsq))
                dve.wait_ge(gain_in, 16 * (n + 1))
                for s in range(S):
                    ins = V.scalar_tensor_tensor(out=normed[:, s, :], in0=X[:, s, :], scalar=rstd[:, s:s + 1],
                                                 in1=gain[:, :], op0=ALU.mult, op1=ALU.mult)
                    if final:
                        ins.then_inc(h_ready, 1)
                    else:
                        st.mark(ins)
                if final:
                    return
                st.wait()
                V.tensor_copy(small[:, 151:152], rstd[:, 0:1]).then_inc(gain_used, 1)
                for s in range(S):
                    dve.wait_ge(bc_done, 2 * n + s + 1)
                    hv = H[:, s, :, :].rearrange("t k p -> t p k")
                    nv = normed[:, s, :].rearrange("t (p k) -> t p k", k=KT)
                    for half in range(2):
                        psv = PS[:, 2 * s + half, :].rearrange("t (p k) -> t p k", k=KT)
                        st.mark(V.scalar_tensor_tensor(out=nv[:, 64 * half:64 * half + 64, :], in0=psv, scalar=1.0,
                                                       in1=nv[:, 64 * half:64 * half + 64, :],
                                                       op0=ALU.add, op1=ALU.mult))
                    st.wait()
                    for half in range(2):
                        psv = PS[:, 4 + 2 * s + half, :].rearrange("t (p k) -> t p k", k=KT)
                        V.tensor_tensor(hv[:, 64 * half:64 * half + 64, :], nv[:, 64 * half:64 * half + 64, :], psv,
                                        ALU.add).then_inc(h_ready, 1)

            def evac_ht(n):
                for s in range(S):
                    dve.wait_ge(ht_done, 2 * n + s + 1)
                    V.tensor_copy(HT[:, 4:8, P * s:P * s + P], PS[:, 2 * s + 1, :].rearrange("p (k t) -> p k t", k=4))\
                        .then_inc(ht_ready, 1)

            def residual(n):
                if n % 2:
                    dve.wait_ge(branch_done, n // 2 + 1)
                else:
                    dve.wait_ge(used, AT[("even_out", 1) if n == 0 else ("odd_out", 3)] + 1)
                for s in range(S):
                    dve.wait_ge(gate_ready, 2 * n + s + 1)
                    st.link(V.tensor_tensor(gated[:, s, :], PS[:, 2 * s:2 * s + 2, :].rearrange("p b n -> p (b n)"),
                                            gated[:, s, :], ALU.mult))
                    V.tensor_tensor(X[:, s, :], X[:, s, :], gated[:, s, :], ALU.add).then_inc(x_ready, 1)

            V.memset(modrow[:, :, :].bitcast(mybir.dt.uint32), 0).then_inc(pad_clear, 1)
            V.memset(cpad[:, :, :], 0.0).then_inc(pad_clear, 1)
            V.memset(small[:, 150:151], EPS).then_inc(pad_clear, 1)
            dve.wait_ge(c_sig, 1)
            dve.wait_ge(pad_clear, 3)
            V.tensor_tensor(cpad[:, :, 2:2 + S], cvec[:, :, :].rearrange("p s k -> p k s"), csig.rearrange("p s k -> p k s"), ALU.mult).then_inc(c_ready, 1)
            dve.wait_ge(lb_t, 1)
            st.link(V.tensor_copy(lbcol[:, :, :].rearrange("p a b -> p (a b)"), PS[:, 1, 0:24]))
            st.link(V.tensor_tensor(lb[:, 0, :], lbcol[:, 0, :], lbcol[:, 1, :], ALU.max))
            st.link(V.tensor_tensor(lb[:, 0, :], lb[:, 0, :], lbcol[:, 2, :], ALU.max))
            for a in range(3):
                ins = V.tensor_tensor(lbtmp[:, a, :], lbcol[:, a, :], lb[:, 0, :], ALU.subtract)
                if a < 2:
                    st.mark(ins)
            st.wait()
            ins.then_inc(lb_sub, 1)
            dve.wait_ge(lb_exp, 1)
            st.link(V.tensor_tensor(lb[:, 1, :], lbtmp[:, 0, :], lbtmp[:, 1, :], ALU.add))
            st.link(V.tensor_tensor(lb[:, 1, :], lb[:, 1, :], lbtmp[:, 2, :], ALU.add))
            st.link(V.reciprocal(lb[:, 1, :], lb[:, 1, :]))
            st.link(V.tensor_tensor(lb[:, 0, :], lbtmp[:, 0, :], lb[:, 1, :], ALU.mult))
            V.tensor_scalar(lb[:, 1, :], lb[:, 0, :], -1.0, 1.0, ALU.mult, ALU.add).then_inc(lb_ready, 1)
            dve.wait_ge(bias_in, 16 * 8)
            mod_rows(0, 0, 0, 0)
            mod_rows(0, 1, 1, 0)
            norm(0)
            evac_ht(0)

            dve.wait_ge(lb_ready, 1)
            late = list(MOD_LATE)

            def late_mod(k):
                for _ in range(k):
                    l, b = late.pop(0)
                    mod_rows(l, b, 2 + len(MOD_LATE) - len(late) - 1, 5)

            for i, c in enumerate(EVEN_ORDER):
                bank = 2 * (i % 4)
                flat = PS[:, bank:bank + 2, :].rearrange("p b n -> p (b n)")
                byhead = flat.rearrange("p (h t) -> p h t", h=HA)
                dve.wait_ge(used, AT[("even_in", c)] + 1)
                if c in (ZF, ZB):
                    d = 0 if c == ZF else 1
                    dve.wait_ge(f_ready, d + 1)
                    for h in range(HA):
                        j = HA * d + h
                        ins = V.tensor_scalar(LF[:, d, h, :], LF[:, d, h, :], lb[:, 1, j:j + 1], lb[:, 0, j:j + 1],
                                              ALU.mult, ALU.add)
                        if h < HA - 1:
                            st.mark(ins)
                    ins.then_inc(key_ready, 1)
                    dve.wait_ge(in_free_a, i + 1)
                    for h in range(HA):
                        j = HA * d + h
                        ins = V.tensor_scalar(KEYT[:, d, h, :], KEYT[:, d, h, :], lb[:, 1, j:j + 1], None, ALU.mult)
                        if h < HA - 1:
                            st.mark(ins)
                    ins.then_inc(key_ready, 1)
                    st.wait()
                elif c == QA:
                    dve.wait_ge(sg_ready, 1)
                    V.scalar_tensor_tensor(out=QT[:, :, :], in0=byhead, scalar=float(P) ** -0.5, in1=SG[:, :, :],
                                           op0=ALU.mult, op1=ALU.mult).then_inc(in_free_v, 1)
                elif c == IA_:
                    V.tensor_copy(IV[:, 1, :], PS[:, bank + 1, :]).then_inc(in_free_v, 1)
                elif c in (QB, KVB):
                    a = 0 if c == QB else 4
                    V.tensor_copy(QKV[:, 1, a:a + 4, :], PS[:, bank + 1, :].rearrange("p (a b) -> p a b", a=4))\
                        .then_inc(in_free_v, 1)
                else:
                    dve.wait_ge(gs_act, 1)
                    dve.wait_ge(cast_done, 16 * 12)
                    V.tensor_tensor(GS[:, :, :], GS[:, :, :], bcast(GNA.unsqueeze(1), [P, S, 512]), ALU.mult)\
                        .then_inc(gs_ready, 1)
            dve.wait_ge(in_free_v, 4)
            dve.wait_ge(key_ready, 4)
            dve.wait_ge(gs_ready, 1)
            for g in range(4):
                s, d = g // 2, g % 2
                ts = slice(P * s, P * s + P)
                dve.wait_ge(lft_done, g + 1)
                if g:
                    dve.wait_ge(group_done, g)
                V.tensor_copy(LFT[:, :, :].rearrange("p h k -> p (h k)"), PS[:, 4, :]).then_inc(lft_ready, 1)
                late_mod(2)
                dve.wait_ge(exps_ready, 3 * g + 3)
                last = SUB - 1 if d == 0 else 0
                st.link(V.tensor_copy(DEC, E23[:, :, last:P:SUB]))
                V.tensor_tensor(E1[:, :, :], E1[:, :, :], QT[:, :, ts], ALU.mult).then_inc(qk_ready, 1)
                V.tensor_tensor(E1N[:, :, :], E1N[:, :, :], KEYT[:, d, :, ts], ALU.mult).then_inc(qk_ready, 1)
                V.tensor_tensor(E23[:, :, 0:P], E23[:, :, 0:P], QT[:, :, ts], ALU.mult).then_inc(qk_ready, 1)
                V.tensor_tensor(E23[:, :, P:2 * P], E23[:, :, P:2 * P], KEYT[:, d, :, ts], ALU.mult)\
                    .then_inc(qk_ready, 1)
                dve.wait_ge(scores_done, g + 1)
                V.tensor_tensor(LFT[:, :, :], PS[:, 4, :].rearrange("p (h k) -> p h k", h=HA),
                                bcast(cums_c[:, d, P:2 * P].unsqueeze(1), [P, HA, P]), ALU.mult).then_inc(pt_ready, 1)
                dve.wait_ge(kv_done, g + 1)
                if g:
                    dve.wait_ge(state_out, 16 * min(g, 2))
                dve.wait_ge(cast_done, 16 * 12)
                order = list(range(NSUB)) if d == 0 else list(range(NSUB))[::-1]
                for i, n in enumerate(order):
                    if s == 1 and i == NSUB - 1:
                        break
                    new = ST[:, i, :]
                    if s == 0 and i == 0:
                        st.link(V.tensor_copy(new, PS[:, n, :]))
                        continue
                    old = S0A[:, d, :] if i == 0 else ST[:, i - 1, :]
                    st.link(V.tensor_tensor(new.rearrange("p (h v) -> p h v", h=HA),
                                            old.rearrange("p (h v) -> p h v", h=HA),
                                            bcast(DEC[:, :, n:n + 1], [P, HA, P]), ALU.mult))
                    st.link(V.tensor_tensor(new, new, PS[:, n, :], ALU.add))
                V.tensor_copy(small[:, 151:152], small[:, 150:151]).then_inc(states_ready, 1)
            dve.wait_ge(oa_std, 1)
            st.link(V.reciprocal(rsA, ssA))
            for s in range(S):
                for h in range(HA):
                    j = HA * s + h
                    gsv = GS[:, s, P * h:P * h + P]
                    ins = V.scalar_tensor_tensor(out=gsv, in0=PS[:, 6 + s, P * h:P * h + P], scalar=rsA[:, j:j + 1],
                                                 in1=gsv, op0=ALU.mult, op1=ALU.mult)
                    if h < HA - 1:
                        st.mark(ins)
                st.wait()
                ins.then_inc(oa_ready, 1)
            dve.wait_ge(group_done, 4)
            for s in range(S):
                st.link(V.tensor_tensor(SQ[:, s, :, :],
                                        QKV[:, s, 0:6, :], QKV[:, s, 0:6, :], ALU.mult))
                V.tensor_reduce(ssB[:, 6 * s:6 * s + 6], SQ[:, s, :, :], AX, ALU.add).then_inc(b_ss, 1)
            dve.wait_ge(b_std, 1)
            st.link(V.reciprocal(rsB, ssB))
            for s in range(S):
                qk = QKV[:, s, 0:6, :]
                st.link(V.tensor_tensor(qk, qk, bcast(rsB[:, 6 * s:6 * s + 6].unsqueeze(2), [P, 6, P]), ALU.mult))
                st.mark(V.tensor_tensor(QKV[:, s, 0:4, :], QKV[:, s, 0:4, :],
                                        bcast(QNG[:, 0, :].unsqueeze(1), [P, 4, P]), ALU.mult))
                st.link(V.tensor_tensor(QKV[:, s, 4:6, :], QKV[:, s, 4:6, :],
                                        bcast(QNG[:, 1, :].unsqueeze(1), [P, 2, P]), ALU.mult))
                if s:
                    c_, s_ = (bcast(cst(x).unsqueeze(1), [P, 6, 64]) for x in ("cosb", "sinb"))
                    x1, x2 = QKV[:, s, 0:6, 0:64], QKV[:, s, 0:6, 64:128]
                    st.mark(V.tensor_tensor(SQf[:, 0, :, :], x1, c_, ALU.mult))
                    st.mark(V.tensor_tensor(SQf[:, 1, :, :], x2, s_, ALU.mult))
                    st.mark(V.tensor_tensor(SQf[:, 2, :, :], x2, c_, ALU.mult))
                    st.link(V.tensor_tensor(SQf[:, 3, :, :], x1, s_, ALU.mult))
                    st.mark(V.tensor_tensor(x1, SQf[:, 0, :, :], SQf[:, 1, :, :], ALU.subtract))
                    st.link(V.tensor_tensor(x2, SQf[:, 2, :, :], SQf[:, 3, :, :], ALU.add))
                V.tensor_copy(small[:, 151:152], small[:, 150:151]).then_inc(b_ready, 1)
            for s in range(S):
                nk = 1 + s
                late_mod(1)
                dve.wait_ge(bs_done, s + 1)
                src = PS[:, 2:4, :].rearrange("p b n -> p (b n)")[:, 0:HB * P * nk].rearrange("p (h t) -> p h t", h=HB)
                st.link(V.tensor_reduce(mxB, src, AX, ALU.max))
                V.tensor_scalar(nbB, mxB, -(float(P) ** -0.5), None, ALU.mult).then_inc(b_max, 1)
                dve.wait_ge(b_exp, HB * (s + 1))
                st.link(V.reciprocal(riB, smB))
                prv = PR[:, :, 0:P * nk]
                V.tensor_tensor(prv, prv, bcast(riB.unsqueeze(2), [P, HB, P * nk]), ALU.mult).then_inc(b_prob, 1)
            residual(0)

            def moe(l):
                ov = OV[l]
                dve.wait_ge(out_sem, 32)
                dve.wait_ge(state_out, 32)
                dve.wait_ge(logit_done, l + 1)
                st.link(V.tensor_copy(LGT[:, :, :], PS[:, 4, 0:128].rearrange("p (s n) -> p s n", s=S)[:, :, 0:NG + NE]))
                lg4 = LGT[:, :, 0:NG]
                g4 = [G4[:, i, :].rearrange("p (s g) -> p s g", s=S) for i in range(3)]
                gmax, gsum, prob = s1[:, 0:2], s1[:, 2:4], s1[:, 4:6]
                st.link(V.tensor_reduce(gmax, lg4, AX, ALU.max))
                gm = bcast(gmax.unsqueeze(2), [P, S, NG])
                st.mark(V.tensor_tensor(g4[0], lg4, gm, ALU.is_equal))
                V.tensor_tensor(g4[1], lg4, gm, ALU.subtract).then_inc(r_gexp_in, 1)
                st.wait()
                st.link(V.tensor_tensor(g4[0], g4[0], bcast(cst("tie4").unsqueeze(1), [P, S, NG]), ALU.mult))
                st.link(V.tensor_reduce(s1[:, 6:8], g4[0], AX, ALU.max))
                st.link(V.tensor_tensor(g4[0], g4[0], bcast(s1[:, 6:8].unsqueeze(2), [P, S, NG]), ALU.is_equal))
                dve.wait_ge(r_gexp, l + 1)
                st.link(V.tensor_reduce(gsum, g4[1], AX, ALU.add))
                st.mark(V.reciprocal(prob, gsum))
                lge = LGT[:, :, NG:].rearrange("p s (g e) -> p s g e", g=NG)
                for s in range(S):
                    st.mark(V.tensor_tensor(PRD[:, NG * s:NG * s + NG, :], lge[:, s, :, :],
                                            bcast(g4[0][:, s, :].unsqueeze(2), [P, NG, EG]), ALU.mult))
                st.wait()
                e8 = [E8[:, i, :].rearrange("p (s e) -> p s e", s=S) for i in range(8)]
                for s in range(S):
                    st.mark(V.tensor_reduce(e8[0][:, s, :], PRD[:, NG * s:NG * s + NG, :].rearrange("p g e -> p e g"),
                                            AX, ALU.add))
                st.wait()
                tie = bcast(cst("tie8").unsqueeze(1), [P, S, EG])

                def top(logits, m, hot):
                    st.link(V.tensor_reduce(m, logits, AX, ALU.max))
                    st.link(V.tensor_tensor(hot, logits, bcast(m.unsqueeze(2), [P, S, EG]), ALU.is_equal))
                    st.link(V.tensor_tensor(hot, hot, tie, ALU.mult))
                    st.link(V.tensor_reduce(s1[:, 12:14], hot, AX, ALU.max))
                    st.link(V.tensor_tensor(hot, hot, bcast(s1[:, 12:14].unsqueeze(2), [P, S, EG]), ALU.is_equal))

                m1, m2 = s1[:, 14:16], s1[:, 16:18]
                top(e8[0], m1, e8[1])
                st.link(V.scalar_tensor_tensor(out=e8[2], in0=e8[1], scalar=-BIG, in1=e8[0],
                                               op0=ALU.mult, op1=ALU.add))
                top(e8[2], m2, e8[3])
                V.tensor_tensor(s1[:, 8:10], m2, m1, ALU.subtract).then_inc(r_exp_in, 1)
                dve.wait_ge(r_exp, l + 1)
                w1, w2 = s1[:, 18:20], s1[:, 20:22]
                st.link(V.tensor_scalar(w1, s1[:, 8:10], 1.0, None, ALU.add))
                st.link(V.reciprocal(w1, w1))
                st.link(V.tensor_tensor(w1, w1, prob, ALU.mult))
                st.link(V.tensor_tensor(w2, w1, s1[:, 8:10], ALU.mult))
                st.mark(V.tensor_tensor(e8[4], e8[1], bcast(w1.unsqueeze(2), [P, S, EG]), ALU.mult))
                st.mark(V.tensor_tensor(e8[5], e8[3], bcast(w2.unsqueeze(2), [P, S, EG]), ALU.mult))
                st.link(V.tensor_tensor(e8[6], e8[1], e8[3], ALU.add))
                st.link(V.tensor_tensor(e8[4], e8[4], e8[5], ALU.add))
                st.mark(V.memset(CW[:, :, NE:], 0.0))
                st.mark(V.memset(POS[:, :, NE:], -1.0))
                for s in range(S):
                    gh = bcast(g4[0][:, s, :].unsqueeze(2), [P, NG, EG])
                    st.mark(V.tensor_tensor(CW[:, s, 0:NE].rearrange("p (g e) -> p g e", g=NG), gh,
                                            bcast(e8[4][:, s, :].unsqueeze(1), [P, NG, EG]), ALU.mult))
                    st.mark(V.tensor_tensor(MASK[:, s, :].rearrange("p (g e) -> p g e", g=NG), gh,
                                            bcast(e8[6][:, s, :].unsqueeze(1), [P, NG, EG]), ALU.mult))
                st.wait()
                V.tensor_copy(small[:, 151:152], small[:, 150:151]).then_inc(mask_ready, 1)
                dve.wait_ge(prefix_done, l + 1)
                pre = PS[:, 5, 0:128].rearrange("p (s n) -> p s n", s=S)[:, :, 0:NE]
                pos = POS[:, :, 0:NE]
                st.link(V.tensor_scalar(pos, pre, 1.0, None, ALU.add))
                st.link(V.tensor_tensor(pos, pos, MASK[:, :, :], ALU.mult))
                st.link(V.tensor_scalar(pos, pos, -1.0, None, ALU.add))
                st.link(V.tensor_reduce(s1[:, 22:23], PS[:, 5, 128:128 + NE], AX, ALU.max))
                V.tensor_copy(CNT[:, 0:1], s1[:, 22:23]).then_inc(count_ready, 1)

                def build(p, par, sel_sig, wsel_sig):
                    for s in range(S):
                        ins = V.tensor_tensor(
                            SEL[:, par, s, :].rearrange("p (e c) -> p e c", e=2),
                            bcast(cst("slots").unsqueeze(1), [P, 2, CAP]),
                            bcast(POS[:, s, bass.ds(p * 2, 2)].unsqueeze(2), [P, 2, CAP]), ALU.is_equal)
                        if s == 0:
                            ins.then_inc(sel_sig, 1)
                    ins.then_inc(sel_sig, 1)

                def weigh(p, par, wsel_sig):
                    for s in range(S):
                        V.tensor_tensor(
                            WSEL[:, par, s, :].rearrange("p (e c) -> p e c", e=2),
                            SEL[:, par, s, :].rearrange("p (e c) -> p e c", e=2),
                            bcast(CW[:, s, bass.ds(p * 2, 2)].unsqueeze(2), [P, 2, CAP]), ALU.mult)\
                            .then_inc(wsel_sig, 1)

                def select(p, par):
                    build(p, par, sel_ready, None)
                    dve.wait_ge(sel_ready, p * 2 + (34 * l + 2))
                    weigh(p, par, wsel_ready)

                def xg_half(half, par):
                    return V.tensor_copy(XG[:, par, 4 * half:4 * half + 4, :].rearrange("p k t -> p (k t)"),
                                         PS[:, 4 + half, :])

                def pair(p, par, last=False):
                    t = p + 16 * l
                    dve.wait_ge(silu_ready, t + 1)
                    V.tensor_tensor(ACTB, PS[:, 6, FE:2 * FE], SILB, ALU.mult).then_inc(act_ready, 1)
                    if not last:
                        dve.wait_ge(gather1_done, t + 2)
                        xg_half(1, 1 - par).then_inc(xg1_ready, 1)
                        select(p + 2, par)
                    dve.wait_ge(down0_done, t + 1)
                    V.tensor_copy(YG[:, 0, :], PS[:, 4, :]).then_inc(yg0_ready, 1)

                select(0, 0)
                select(1, 1)
                dve.wait_ge(gather1_done, 16 * l + 1)
                xg_half(1, 0).then_inc(xg1_ready, 1)
                pair(0, 0)
                with dve.Fori(0, NPAIR // 2 - 1) as i:
                    pair(i * 2 + 1, 1)
                    pair(i * 2 + 2, 0)
                pair(NPAIR - 1, 1, last=True)
                dve.wait_ge(count_ready, l + 1)
                most = dve.value_load(CNT[0:1, 0:1], min_val=0, max_val=S * P)
                with dve.If(most > CAP):
                    with dve.Fori(0, ROUNDS - 1) as r:
                        V.tensor_scalar(POS[:, :, :], POS[:, :, :], -float(CAP), None, ALU.add).then_inc(ov["shift"], 1)
                        with dve.Fori(0, NPAIR) as p:
                            t = r * NPAIR + p
                            dve.wait_ge(ov["scat"], t)
                            dve.wait_ge(ov["shift"], r + 1)
                            build(p, 0, ov["sel"], None)
                            dve.wait_ge(ov["sel"], t * 4 + 2)
                            weigh(p, 0, ov["sel"])
                            dve.wait_ge(ov["sil"], t + 1)
                            V.tensor_tensor(ACTB, PS[:, 6, FE:2 * FE], SILB, ALU.mult).then_inc(ov["act"], 1)
                residual(2 * l + 1)

            norm(1)
            evac_ht(1)
            moe(0)
            norm(2)
            evac_ht(2)
            def evac_odd(c, i):
                bank = 2 * (i % 4)
                dve.wait_ge(used, AT[("odd_in", c)] + 1)
                dst = QKc[:, 1, 512 * c:512 * c + 512] if c < 4 else VY[:, 1, 512 * (c - 4):512 * (c - 4) + 512]
                V.tensor_copy(dst, PS[:, bank + 1, :]).then_inc(c_free_v, 1)

            for c in range(8):
                evac_odd(c, c)
            dve.wait_ge(c_free_a, 8)
            dve.wait_ge(c_free_v, 8)
            for s in range(S):
                st.mark(V.tensor_scalar(QKc[:, s, 1024:2048], QKc[:, s, 1024:2048], float(2 * P) ** -0.5, None, ALU.mult))
            st.wait()
            for h in range(HC):
                dve.wait_ge(c_pow, 2 * h + 2)
                st.mark(V.tensor_tensor(LGP[:, 0, :], LGP[:, 0, :], cst("ge"), ALU.mult))
                st.link(V.tensor_tensor(LGP[:, 1, :], LGP[:, 1, :], cst("le"), ALU.mult))
                V.tensor_tensor(DM[:, h, :], LGP[:, 0, :], LGP[:, 1, :], ALU.add).then_inc(c_dm, 1)
            dve.wait_ge(c_dm, HC)
            dve.wait_ge(a_step, ACT_STEPS_KD)
            xq = QKc[:, 1, :].rearrange("p (n c) -> p n c", n=8)
            c_, s_ = (bcast(cst(x).unsqueeze(1), [P, 4, P]) for x in ("cosc", "sinc"))
            tmp = SF[:, :, :].rearrange("p a (n c) -> p a n c", n=4)
            for part in range(2):
                x1, x2 = xq[:, 4 * part:4 * part + 4, 0:P], xq[:, 4 * part:4 * part + 4, P:2 * P]
                st.mark(V.tensor_tensor(tmp[:, 0, :, :], x1, c_, ALU.mult))
                st.mark(V.tensor_tensor(tmp[:, 1, :, :], x2, s_, ALU.mult))
                st.mark(V.tensor_tensor(tmp[:, 2, :, :], x2, c_, ALU.mult))
                st.link(V.tensor_tensor(tmp[:, 3, :, :], x1, s_, ALU.mult))
                st.mark(V.tensor_tensor(x1, tmp[:, 0, :, :], tmp[:, 1, :, :], ALU.subtract))
                st.link(V.tensor_tensor(x2, tmp[:, 2, :, :], tmp[:, 3, :, :], ALU.add))
            V.tensor_copy(small[:, 151:152], small[:, 150:151]).then_inc(c_rope, 1)
            for s in range(S):
                for h in range(HC):
                    u = HC * s + h
                    if s == 0:
                        if h:
                            dve.wait_ge(cstate_done, 4 * h)
                        for d in range(2):
                            V.tensor_scalar(KD[:, d, :], QKc[:, 0, 1024 + 256 * h:1024 + 256 * h + 256],
                                            KDC[:, HC * d + h:HC * d + h + 1], None, ALU.mult).then_inc(kd_ready, 1)
                    dve.wait_ge(cs_done, u + 1)
                    if u:
                        dve.wait_ge(co_done, u)
                    V.tensor_tensor(PC, PS[:, 1, 0:P], DM[:, h, :], ALU.mult).then_inc(cp_ready, 1)
                    if s:
                        dve.wait_ge(c_pow, 2 * HC + 2 * (h + 1))
                        for d in range(2):
                            ins = V.tensor_tensor(QD[:, 2 * d:2 * d + 2, :], TT[:, 0:2, :],
                                                  bcast(LGP[:, d, :].unsqueeze(1), [P, 2, P]), ALU.mult)
                            st.link(ins)
                        V.tensor_copy(small[:, 151:152], small[:, 150:151]).then_inc(cd_ready, 1)
                    dve.wait_ge(co_done, u + 1)
                    st.link(V.bn_stats(bnC[:, s, h, :], PS[:, 2, :]))
                    V.bn_aggr(mvC[:, u, :], bnC[:, s, h, :]).then_inc(c_std, 1)
                    dve.wait_ge(c_std, 2 * u + 2)
                    st.link(V.reciprocal(rsC[:, u:u + 1], sdC[:, u:u + 1]))
                    V.tensor_scalar(VY[:, s, VC * h:VC * h + VC], PS[:, 2, :], mvC[:, u, 0:1], rsC[:, u:u + 1],
                                    ALU.subtract, ALU.mult).then_inc(c_y, 1)
            dve.wait_ge(gn_in, 16)
            dve.wait_ge(c_y, 2 * HC)
            for s in range(S):
                st.mark(V.tensor_tensor(VY[:, s, :], VY[:, s, :], GNC, ALU.mult))
            st.wait()
            for i in range(4):
                dve.wait_ge(g_act, i + 1)
                for s in range(S):
                    yv = VY[:, s, 512 * i:512 * i + 512]
                    V.tensor_tensor(yv, yv, SF[:, s, :], ALU.mult).then_inc(g_ready, 1)
            residual(2)
            norm(3)
            evac_ht(3)
            moe(1)
            norm(4, final=True)


ACT_STEPS_KD = 1 + 8 + 8


def shape_constants(np):
    c = np.zeros((P, NCONST), np.float32)

    def put(name, v):
        a, b = CONST_AT[name]
        c[:, a:b] = np.asarray(v, np.float32).reshape(P, b - a)

    t = np.arange(P)
    a, b = t[:, None], t[None, :]
    same = (a // SUB) == (b // SUB)
    put("ident", a == b)
    mid_f, mid_b = (b // SUB) * SUB + SUB // 2 - 1, (b // SUB) * SUB + SUB // 2
    fwd = [1.0 * (same & (a <= b)) - 1.0 * (same & (a <= mid_f)), 1.0 * (same & (a <= b)), 1.0 * (same & (a > b))]
    bwd = [1.0 * (same & (a >= b)) - 1.0 * (same & (a >= mid_b)), 1.0 * (same & (a >= b)), 1.0 * (same & (a < b))]
    put("cums", np.concatenate(fwd + bwd, 1))
    put("relp", np.maximum(b - a, 0))
    put("relm", np.maximum(a - b, 0))
    put("ge", b >= a)
    put("le", b <= a)
    put("powers", np.stack([t + 1, P - t, P - 1 - t, t], 1))
    put("rowf", np.broadcast_to(t + 1, (P, P)))
    put("rowb", np.broadcast_to(P - t, (P, P)))
    row, col = (t // 64).astype(np.float32), (t % 64).astype(np.float32)
    for width, cn, sn in ((128, "cosb", "sinb"), (256, "cosc", "sinc")):
        nf = width // 4
        inv = (10000.0 ** (-np.arange(nf, dtype=np.float64) / nf)).astype(np.float32)
        ang = np.concatenate([row[:, None] * inv, col[:, None] * inv], 1)
        put(cn, np.cos(ang.astype(np.float64)))
        put(sn, np.sin(ang.astype(np.float64)))
    put("upper", a < b)
    put("ones", np.ones((P, P)))
    put("slots", np.broadcast_to(np.arange(CAP), (P, CAP)))
    sel = np.zeros((P, 2, S, 2, P))
    for l in range(2):
        for s in range(S):
            for half in range(2):
                for parity in range(2):
                    sel[32 * (2 * parity + half) + 2 * l + s, l, s, half, :] = 1
    put("selb", sel)
    put("tie4", np.broadcast_to(NG - np.arange(NG), (P, NG)))
    put("tie8", np.broadcast_to(EG - np.arange(EG), (P, EG)))
    return c


_INS = ["x_prompt", "x_sample", "cache_attn_k", "cache_attn_v", "state_hgrn", "state_ret", "c", "c_ctx",
        "mod_w", "mod_b", "norm1_g", "norm2_g", "even_w_in", "even_w_out", "hgrn_lb_logits", "hgrn_norm_g",
        "attn_qn_g", "attn_kn_g", "odd_w_in", "odd_w_out", "ret_decay_logit", "ret_gn_g",
        "moe_w_group", "moe_b_group", "moe_w_expert", "moe_b_expert", "moe_w_gate", "moe_w_up", "moe_w_down",
        "final_norm_g"]
_OUTS = [("y_prompt", (1, P, D)), ("y_sample", (1, P, D)), ("new_attn_k", (1, 1, P, KVH, P)),
         ("new_attn_v", (1, 1, P, KVH, P)), ("new_state_hgrn", (1, 1, 2, HA, P, P)),
         ("new_state_ret", (1, 1, 2, HC, 2 * P, VC))]


def kernel(**inputs):
    import numpy as np
    import concourse.bacc as bacc
    from concourse.bass_utils import run_bass_kernel_spmd as run

    nc = bacc.Bacc("TRN2", target_bir_lowering=False, num_devices=1)
    arrays, ins, outs = {}, {}, {}
    for name in _INS:
        a = np.ascontiguousarray(inputs[name])
        arrays[f"in_{name}"] = a
        ins[name] = nc.dram_tensor(f"in_{name}", a.shape, F32, kind="ExternalInput").ap()
    arrays["in_consts"] = shape_constants(np)
    ins["consts"] = nc.dram_tensor("in_consts", (P, NCONST), F32, kind="ExternalInput").ap()
    for name, shape in _OUTS:
        outs[name] = nc.dram_tensor(f"out_{name}", shape, F32, kind="ExternalOutput").ap()
    backbone(nc, ins, outs)
    r = run(nc, [arrays], core_ids=[0])
    return tuple(r.results[0][f"out_{name}"] for name, _ in _OUTS)
```

```python
from contextlib import ExitStack

import concourse.bass as bass
from concourse import mybir
from concourse.alu_op_type import AluOpType as ALU

ACT = mybir.ActivationFunctionType
AX = mybir.AxisListType.X
F32 = mybir.dt.float32
I32 = mybir.dt.int32
SIGMOID, SILU, EXP, LN, SQRT, SQUARE, COPY = (
    ACT.Sigmoid, ACT.Silu, ACT.Exp, ACT.Ln, ACT.Sqrt, ACT.Square, ACT.Copy)

P = 128
S = 2
D = 1024
KT = D // P
EPS = 1e-6
BANK = 512
SUB = 32
NSUB = P // SUB
HA = 4
HB = 4
KVH = 2
HC = 4
VC = 512
NG, EG = 4, 8
NE = NG * EG
FE = 256
CAP = 64
NPAIR = NE // 2
ROUNDS = S * P // CAP
RING = 6
SLOT = 4096
MB = 6
BIG = 1.0e30

CONST_PARTS = [
    ("ident", P), ("selb", 2 * S * 2 * P), ("cums", 2 * 3 * P), ("relp", P), ("relm", P), ("ge", P), ("le", P),
    ("powers", 4), ("rowf", P), ("rowb", P), ("cosb", 64), ("sinb", 64), ("cosc", P), ("sinc", P), ("upper", P),
    ("ones", P), ("slots", CAP), ("tie4", NG), ("tie8", EG)]
CONST_AT = {}
_n = 0
for _name, _w in CONST_PARTS:
    CONST_AT[_name] = (_n, _n + _w)
    _n += _w
NCONST = _n
NFIRST = CONST_AT["cums"][0]

QA, IA_, ZF, ZB, GA, QB, KVB = range(7)
EVEN_ORDER = [ZF, ZB, QA, IA_, QB, KVB, GA]
PREP_BANK = [6, 0, 2, 6]
MOD_BANK = {1: 7, 2: 7, 3: 3}


def weight_stream():
    items = [("mod", 0, b, q) for b in (1, 0) for q in (0, 1)]
    late = list(MOD_LATE)
    for i, c in enumerate(EVEN_ORDER):
        items.append(("even_in", c))
        if i in MOD_BANK:
            l, b = late.pop(0)
            items += [("mod", l, b, 0), ("mod", l, b, 1)]
    items += [("mod", l, b, q) for l, b in late for q in (0, 1)]
    items += [("even_out", q) for q in range(2)]
    items += [("moe", 0, p, m) for p in range(NPAIR) for m in range(3)]
    items += [("odd_in", c) for c in range(12)]
    items += [("state", d) for d in range(2)]
    items += [("odd_out", q) for q in range(4)]
    items += [("moe", 1, p, m) for p in range(NPAIR) for m in range(3)]
    return items


ODD_HALVES = ([(c, s) for c in (5, 6, 7) for s in (0, 1)] + [(c, 0) for c in (8, 9, 10, 11)]
              + [(c, 1) for c in (8, 9, 10, 11)])
HEAD_HALVES = [ODD_HALVES[2 * u:2 * u + 2] for u in range(5)] + [ODD_HALVES[u + 5:u + 6] for u in range(5, 8)]

MOD_LATE = [(0, b) for b in range(2, MB)] + [(1, b) for b in range(MB)]
STREAM = weight_stream()
AT = {item: n for n, item in enumerate(STREAM)}


def backbone(nc, A, O):
    ctx = ExitStack()
    with ctx:
        def sb(name, shape, dt=F32):
            return ctx.enter_context(nc.sbuf_tensor(name, shape, dt))

        def sem(name):
            return ctx.enter_context(nc.semaphore(name))

        ring = sb("ring", [P, RING, SLOT])
        const = sb("const", [P, NCONST])
        X = sb("X", [P, S, D])
        H = sb("H", [P, S, KT, P])
        HT = sb("HT", [P, 8, S * P])
        modrow = sb("modrow", [P, MB, BANK])
        gain = sb("gain", [P, D])
        scratch = sb("scratch", [P, 11264])
        cvec = sb("cvec", [P, S, KT])
        cpad = sb("cpad", [P, KT, 36])
        lbcol = sb("lbcol", [P, 3, 8])
        lbtmp = sb("lbtmp", [P, 3, 8])
        lb = sb("lb", [P, 2, 8])
        small = sb("small", [P, 160])
        csig = small[:, 120:136].rearrange("p (s k) -> p s k", s=S)
        PS = ctx.enter_context(nc.psum_tensor("PS", [P, 8, BANK], F32))

        def cst(name):
            a, b = CONST_AT[name]
            return const[:, a:b]

        ident = cst("ident")
        cums_c = cst("cums").rearrange("p (d n) -> p d n", d=2)
        zero = cums_c[0:1, 0, 2 * P:3 * P]
        selb_c = cst("selb").rearrange("p (l s h t) -> p l s h t", l=2, s=S, h=2)
        powers_c = cst("powers")

        def carve(at, *shape):
            n = 1
            for x in shape:
                n *= x
            v = scratch[:, at:at + n]
            if len(shape) == 2:
                v = v.rearrange("p (a b) -> p a b", a=shape[0])
            if len(shape) == 3:
                v = v.rearrange("p (a b c) -> p a b c", a=shape[0], b=shape[1])
            return v, at + n

        lbrow = scratch[0:24, 11264 - P:11264]
        normed, _at = carve(0, S, D)
        squares, _at = carve(_at, S, D)
        GATE, _at = carve(11264 - 2 * S * D, S, D)
        GAIN, _at = carve(_at, S, D)
        sumsq, rstd = small[:, 0:2], small[:, 2:4]

        QT, _at = carve(0, HA, S * P)
        IV, _at = carve(_at, S, 512)
        KEYT, _at = carve(_at, 2, HA, S * P)
        GS, _at = carve(_at, S, 512)
        QKV, _at = carve(_at, S, 8, P)
        LFT, _at = carve(_at, HA, P)
        K2, _at = carve(_at, HA, P)
        ST, _at = carve(_at, 4, 512)
        S0A, _at = carve(_at, 2, 512)
        _evend = _at
        LF = H[:, :, :, :].rearrange("p s k c -> p (s k c)").rearrange("p (d h t) -> p d h t", d=2, h=HA)
        SG = ST.rearrange("p a n -> p (a n)")[:, 0:1024].rearrange("p (h t) -> p h t", h=HA)
        assert _evend <= 11264
        E = sb("E", [P, 4 * BANK])
        E1 = E[:, 0:512].rearrange("p (h k) -> p h k", h=HA)
        E1N = E[:, 512:1024].rearrange("p (h k) -> p h k", h=HA)
        E23 = E[:, 1024:2048].rearrange("p (h k) -> p h k", h=HA)
        DEC = small[:, 8:24].rearrange("p (h n) -> p h n", h=HA)
        GNA = gain[:, 0:512]
        QNG = sb("QNG", [P, 2, P])
        CKV = sb("CKV", [P, 2, 2 * P])
        ssA, rsA = small[:, 24:32], small[:, 32:40]
        AT_ = [scratch[:, a:a + n * P].rearrange("p (a c) -> p a c", c=P)
               for a, n in ((0, 6), (1024, 8))]
        PR = [scratch[:, a:a + n * P].rearrange("p (h c) -> p h c", h=HB)
              for a, n in ((7168, 4), (2048, 8))]
        PRT = [scratch[:, a:a + n * P].rearrange("p (a c) -> p a c", c=P)
               for a, n in ((7680, 4), (3072, 8))]
        LFV = LF.rearrange("p d h t -> p (d h) t")[:, :, 0:P]
        ssB, rsB = small[:, 40:52], small[:, 52:64]
        mxB, nbB, smB, riB = ([small[:, a + 4 * i:a + 4 * i + 4] for a in (64, 104)] for i in range(4))

        QKc, _at = carve(0, S, 2048)
        VY, _at = carve(_at, S, 2048)
        DM, _at = carve(_at, HC, P)
        TT, _at = carve(_at, 4, P)
        QD, _at = carve(_at, 4, P)
        PC, _at = carve(_at, P)
        KD, _at = carve(_at, 2, 2 * P)
        LGP, _at = carve(_at, 2, P)
        GB, _at = carve(_at, BANK)
        bnC, _at = carve(_at, S, HC, 6)
        mvC, _at = carve(_at, S * HC, 2)
        assert _at <= 11264, _at
        MIXC = QKc.rearrange("p s n -> p (s n)").rearrange("p (k t) -> p k t", k=16)
        GNC = H[:, :, :, :].rearrange("p s k c -> p (s k c)")
        SF = E[:, :].rearrange("p (a v) -> p a v", a=4)
        LG = small[:, 80:88]
        KDC = small[:, 88:104]
        sdC, rsC = small[:, 104:112], small[:, 112:120]

        XG, _at = carve(0, 2, KT, P)
        SEL, _at = carve(_at, 2, S, P)
        WSEL, _at = carve(_at, 2, S, P)
        WSELT, _at = carve(_at, 2, S, P)
        SILB, _at = carve(_at, FE)
        ACTB, _at = carve(_at, FE)
        ACTT, _at = carve(_at, 2, P)
        YG, _at = carve(_at, 2, BANK)
        LGT, _at = carve(_at, S, NG + NE)
        G4, _at = carve(_at, 3, S * NG)
        PRD, _at = carve(_at, S * NG, EG)
        E8, _at = carve(_at, 8, S * EG)
        LTS = scratch[0:NG + NE, _at:_at + S * P]
        _at += S * P
        MASK, _at = carve(_at, S, NE)
        CW, _at = carve(_at, S, NE + 2)
        POS, _at = carve(_at, S, NE + 2)
        assert _at <= 11264 - 2 * S * D
        s1 = small[:, 120:150]
        RW = sb("RW", [P, KT, NG + NE])
        CNT = sb("CNT", [P, 2], I32)
        rbias = sb("rbias", [1, 2, NG + NE])

        landed = [sem(f"landed{i}") for i in range(RING)]
        used = sem("used")
        params_in = sem("params_in")
        x_in = sem("x_in")
        pad_clear = sem("pad_clear")
        bias_in = sem("bias_in")
        late_params_in = sem("late_params_in")
        start_act = sem("start_act")
        start_dve = sem("start_dve")
        mod_ready = sem("mod_ready")
        lb_turned = sem("lb_turned")
        lb_ready = sem("lb_ready")
        x_ready = sem("x_ready")
        first_gain_in = sem("first_gain_in")
        gain_in = sem("gain_in")
        gain_used = sem("gain_used")
        sq_ready = sem("sq_ready")
        std_ready = sem("std_ready")
        scale_done = sem("scale_done")
        scale_ready = sem("scale_ready")
        shift_done = sem("shift_done")
        prep_done = sem("prep_done")
        prep_read = sem("prep_read")
        h_ready = sem("h_ready")
        ht_done = sem("ht_done")
        ht_ready_a = sem("ht_ready_a")
        ht_ready_v = sem("ht_ready_v")
        v_step = sem("v_step")
        a_step = sem("a_step")
        gate_done = sem("gate_done")
        gate_ready = sem("gate_ready")
        branch_done = sem("branch_done")
        in_free_a = sem("in_free_a")
        in_free_v = sem("in_free_v")
        f_ready = sem("f_ready")
        lf_ready = sem("lf_ready")
        key_ready = sem("key_ready")
        gs_ready = sem("gs_ready")
        half_done = sem("half_done")
        half_read = sem("half_read")
        lft_done = sem("lft_done")
        lft_ready = sem("lft_ready")
        cums_done = sem("cums_done")
        exps_ready = sem("exps_ready")
        qk_ready = sem("qk_ready")
        scores_done = sem("scores_done")
        decayed_turned = sem("decayed_turned")
        masked_ready = sem("masked_ready")
        decayed_ready = sem("decayed_ready")
        kv_done = sem("kv_done")
        states_ready = sem("states_ready")
        group_done = sem("group_done")
        state_out = sem("state_out")
        hgrn_std = sem("hgrn_std")
        hgrn_ready = sem("hgrn_ready")
        hgrn_turned = sem("hgrn_turned")
        mix_ready = sem("mix_ready")
        attn_sq = sem("attn_sq")
        attn_std = sem("attn_std")
        attn_qk_ready = sem("attn_qk_ready")
        attn_qk_turned = sem("attn_qk_turned")
        attn_qkt_ready = sem("attn_qkt_ready")
        attn_scores_done = sem("attn_scores_done")
        attn_max_ready = sem("attn_max_ready")
        attn_exp_ready = sem("attn_exp_ready")
        attn_probs_ready = sem("attn_probs_ready")
        attn_probs_turned = sem("attn_probs_turned")
        attn_probst_ready = sem("attn_probst_ready")
        attn_out_done = sem("attn_out_done")
        out_sem = sem("out_sem")
        y_out = sem("y_out")
        odd_free_a = sem("odd_free_a")
        odd_free_v = sem("odd_free_v")
        decay_ready = sem("decay_ready")
        ret_rope_done = sem("ret_rope_done")
        powers_ready = sem("powers_ready")
        ret_qk_turned = sem("ret_qk_turned")
        ret_qkt_ready = sem("ret_qkt_ready")
        ret_qd_ready = sem("ret_qd_ready")
        ret_scores_done = sem("ret_scores_done")
        ret_masked_ready = sem("ret_masked_ready")
        ret_kd_ready = sem("ret_kd_ready")
        ret_out_done = sem("ret_out_done")
        ret_state_done = sem("ret_state_done")
        ret_state_ready = sem("ret_state_ready")
        ret_state_out = [sem(f"ret_state_out{i}") for i in range(4)]
        ret_stats = sem("ret_stats")
        ret_y_ready = sem("ret_y_ready")
        ret_keys_scaled = sem("ret_keys_scaled")
        odd_half_done = sem("odd_half_done")
        odd_half_read = sem("odd_half_read")
        gated_ready = sem("gated_ready")
        gated_turned = sem("gated_turned")
        odd_mix_ready = sem("odd_mix_ready")
        ret_gain_in = sem("ret_gain_in")
        router_in = sem("router_in")
        logit_sum = sem("logit_sum")
        logit_read = sem("logit_read")
        logit_done = sem("logit_done")
        group_diff = sem("group_diff")
        group_exp = sem("group_exp")
        expert_diff = sem("expert_diff")
        expert_exp = sem("expert_exp")
        mask_ready = sem("mask_ready")
        prefix_done = sem("prefix_done")
        count_ready = sem("count_ready")
        sel_ready = sem("sel_ready")
        wsel_ready = sem("wsel_ready")
        gather0_done = sem("gather0_done")
        gather1_done = sem("gather1_done")
        turn_done = sem("turn_done")
        wselt_ready = sem("wselt_ready")
        actt_ready = sem("actt_ready")
        xg0_ready = sem("xg0_ready")
        xg1_ready = sem("xg1_ready")
        silu_ready = sem("silu_ready")
        act_ready = sem("act_ready")
        down0_done = sem("down0_done")
        yg0_ready = sem("yg0_ready")
        yg1_ready = sem("yg1_ready")
        OV = [{n: sem(f"ov{l}_{n}") for n in
               ("sel", "gath", "xg", "sil", "act", "turn", "actt", "yg", "scat", "in0", "in1", "in2",
                "used", "shift")} for l in range(2)]

        block = ctx.enter_context(nc.Block())

        def slot(item):
            return AT[item] % RING

        def arrived(eng, item):
            n = AT[item]
            eng.wait_ge(landed[n % RING], 16 * (n // RING + 1))

        def bcast(ap, shape):
            return ap.broadcast_to(shape)

        class Steps:

            def __init__(self, eng, s):
                self.eng, self.sem, self.n = eng, s, 0

            def link(self, ins):
                self.mark(ins)
                self.wait()

            def mark(self, ins):
                ins.then_inc(self.sem, 1)
                self.n += 1

            def wait(self):
                self.eng.wait_ge(self.sem, self.n)

        @block.sync
        def _(sp):
            def source(item):
                kind = item[0]
                if kind == "mod":
                    _, l, b, q = item
                    v = A["mod_w"][l].rearrange("(p k) n -> p k n", k=KT)
                    return v[:, 4 * q:4 * q + 4, D * b:D * b + D]
                if kind == "even_in":
                    v = A["even_w_in"][0].rearrange("(p k) n -> p k n", k=KT)
                    return v[:, :, 512 * item[1]:512 * item[1] + 512]
                if kind == "odd_in":
                    v = A["odd_w_in"][0].rearrange("(p k) n -> p k n", k=KT)
                    return v[:, :, 512 * item[1]:512 * item[1] + 512]
                if kind == "state":
                    return A["state_ret"][0, 0, item[1]].rearrange("h (j p) v -> p (h j) v", p=P)
                w = A["even_w_out"] if kind == "even_out" else A["odd_w_out"]
                return w[0].rearrange("(k p) n -> p k n", p=P)[:, 4 * item[1]:4 * item[1] + 4, :]

            def load(n):
                src = source(STREAM[n])
                dst = ring[:, n % RING, :].rearrange("p (a b) -> p a b", b=src.shape[2])
                if n >= RING:
                    sp.wait_ge(used, n - RING + 1)
                sp.dma_start(dst, src).then_inc(landed[n % RING], 16)

            def expert_source(l, m, p):
                if m < 2:
                    w = A["moe_w_gate" if m == 0 else "moe_w_up"][l].rearrange("e (p k) f -> p e (k f)", p=P)
                    return w[:, bass.ds(p * 2, 2), :]
                w = A["moe_w_down"][l].rearrange("e (j p) n -> p (e j) n", p=P)
                return w[:, bass.ds(p * 4, 4), :]

            sp.dma_start(cvec[:, 0, :], A["c_ctx"].rearrange("(p k) -> p k", k=KT)).then_inc(params_in, 16)
            sp.dma_start(cvec[:, 1, :], A["c"][0].rearrange("(p k) -> p k", k=KT)).then_inc(params_in, 16)
            sp.dma_start(lbrow[:, :], A["hgrn_lb_logits"].rearrange("a b (h k) -> (a b h) k", k=P))\
                .then_inc(params_in, 16)
            sp.dma_start(const[:, 0:NFIRST], A["consts"][:, 0:NFIRST]).then_inc(params_in, 16)
            load(0)
            load(1)
            sp.wait_ge(pad_clear, 3)
            for l in range(2):
                mb = A["mod_b"][l].rearrange("(b h n) -> h b n", h=2, n=BANK)
                for half in range(2):
                    for s in range(S):
                        r = 32 * half + 2 * l + s
                        sp.dma_start(modrow[r:r + 1, :, :], mb[half:half + 1]).then_inc(bias_in, 16)
            sp.dma_start(X[:, 0, :], A["x_prompt"][0]).then_inc(x_in, 16)
            sp.dma_start(X[:, 1, :], A["x_sample"][0]).then_inc(x_in, 16)
            sp.dma_start(gain[:, :], A["norm1_g"][0].partition_broadcast(P)).then_inc(first_gain_in, 16)
            load(2)
            load(3)
            sp.wait_ge(params_in, 64)
            sp.dma_start(const[:, NFIRST:], A["consts"][:, NFIRST:]).then_inc(params_in, 16)
            n = 4
            while n < len(STREAM):
                if STREAM[n][0] != "moe":
                    load(n)
                    n += 1
                    continue
                l, first = STREAM[n][1], n
                with sp.Fori(0, NPAIR // 2) as i:
                    for u in range(2):
                        for m in range(3):
                            k = first + 3 * u + m
                            sp.wait_ge(used, i * RING + (k - RING + 1))
                            src = expert_source(l, m, i * 2 + u)
                            dst = ring[:, k % RING, :].rearrange("p (a b) -> p a b", b=src.shape[2])
                            sp.dma_start(dst, src).then_inc(landed[k % RING], 16)
                n += 3 * NPAIR
                sp.wait_ge(count_ready, l + 1)
                most = sp.value_load(CNT[0:1, 0:1], min_val=0, max_val=S * P)
                with sp.If(most > CAP):
                    ov = OV[l]
                    sp.wait_ge(used, n)
                    with sp.Fori(0, ROUNDS - 1) as r:
                        with sp.Fori(0, NPAIR) as p:
                            for m in range(3):
                                sp.wait_ge(ov["used"], (r * NPAIR + p) * 3 + 1)
                                src = expert_source(l, m, p)
                                dst = ring[:, m, :].rearrange("p (a b) -> p a b", b=src.shape[2])
                                sp.dma_start(dst, src).then_inc(ov[f"in{m}"], 16)
                    sp.wait_ge(ov["used"], (ROUNDS - 1) * NPAIR * 3 + 1)

            sp.wait_ge(h_ready, 9)
            sp.dma_start(O["y_prompt"][0], normed[:, 0, :]).then_inc(y_out, 16)
            sp.wait_ge(h_ready, 10)
            sp.dma_start(O["y_sample"][0], normed[:, 1, :]).then_inc(y_out, 16)
            sp.wait_ge(y_out, 32)

        @block.gpsimd
        def _(pool):
            def router_weights(l):
                pool.dma_start(RW[:, :, 0:NG], A["moe_w_group"][l].rearrange("(p k) g -> p k g", k=KT))\
                    .then_inc(router_in, 16)
                pool.dma_start(RW[:, :, NG:], A["moe_w_expert"][l].rearrange("(p k) g -> p k g", k=KT))\
                    .then_inc(router_in, 16)

            router_weights(0)
            pool.dma_start(QNG[:, 0, :], A["attn_qn_g"][0].partition_broadcast(P)).then_inc(late_params_in, 16)
            pool.dma_start(QNG[:, 1, :], A["attn_kn_g"][0].partition_broadcast(P)).then_inc(late_params_in, 16)
            pool.dma_start(CKV[:, 0, :], A["cache_attn_k"][0, 0].rearrange("t h d -> t (h d)")).then_inc(late_params_in, 16)
            pool.dma_start(CKV[:, 1, :], A["cache_attn_v"][0, 0].rearrange("t h d -> t (h d)")).then_inc(late_params_in, 16)
            for l in range(2):
                pool.dma_start(rbias[:, l, 0:NG], A["moe_b_group"][l:l + 1]).then_inc(late_params_in, 16)
                pool.dma_start(rbias[:, l, NG:], A["moe_b_expert"][l:l + 1]).then_inc(late_params_in, 16)
            pool.dma_start(small[:, 80:88], A["ret_decay_logit"][0].rearrange("a b -> (a b)").partition_broadcast(P))\
                .then_inc(late_params_in, 16)

            def next_gain(n, src):
                pool.wait_ge(gain_used, n)
                pool.dma_start(gain[:, :], src.partition_broadcast(P)).then_inc(gain_in, 16)

            pool.wait_ge(h_ready, 2)
            pool.wait_ge(gain_used, 1)
            pool.dma_start(GNA, A["hgrn_norm_g"][0].rearrange("h v -> (h v)").partition_broadcast(P))\
                .then_inc(late_params_in, 16)
            for d in range(2):
                pool.dma_start(S0A[:, d, :].rearrange("p (h v) -> p h v", h=HA),
                               A["state_hgrn"][0, 0, d].rearrange("h k v -> k h v")).then_inc(late_params_in, 16)
            for d in range(2):
                pool.wait_ge(states_ready, d + 1)
                pool.dma_start(O["new_state_hgrn"][0, 0, d].rearrange("h k v -> k h v"),
                               ST[:, 3, :].rearrange("p (h v) -> p h v", h=HA)).then_inc(state_out, 16)
            pool.wait_ge(gs_ready, 1)
            next_gain(1, A["norm2_g"][0])
            pool.wait_ge(attn_qk_ready, 1)
            pool.dma_start(O["new_attn_k"][0, 0].rearrange("t h d -> t (h d)"),
                           QKV[:, 0, 4:6, :].rearrange("p a b -> p (a b)")).then_inc(out_sem, 16)
            pool.dma_start(O["new_attn_v"][0, 0].rearrange("t h d -> t (h d)"),
                           QKV[:, 0, 6:8, :].rearrange("p a b -> p (a b)")).then_inc(out_sem, 16)
            pool.wait_ge(out_sem, 32)
            next_gain(2, A["norm1_g"][1])
            pool.wait_ge(logit_done, 1)
            router_weights(1)
            pool.wait_ge(ht_ready_a, 6)
            pool.wait_ge(ht_ready_v, 6)
            pool.dma_start(GNC, A["ret_gn_g"][0].rearrange("h v -> (h v)").partition_broadcast(P)).then_inc(ret_gain_in, 16)
            next_gain(3, A["norm2_g"][1])
            for n in range(2 * HC * 2):
                pool.wait_ge(ret_state_ready, n + 1)
                h, d, j = n // 4, (n // 2) % 2, n % 2
                pool.dma_start(O["new_state_ret"][0, 0, d, h, P * j:P * j + P, :], SF[:, n % 4, :])\
                    .then_inc(ret_state_out[n % 4], 16)
            for n in range(4):
                pool.wait_ge(ret_state_out[n], 16 * HC)
            next_gain(4, A["final_norm_g"])
            pool.wait_ge(out_sem, 32)
            pool.wait_ge(state_out, 32)

        @block.tensor
        def _(pe):
            def matmul(out, lhsT, rhs, start, stop, **kw):
                return nc.tensor.matmul(out, lhsT, rhs, start=start, stop=stop, skip_group_check=True, **kw)

            def mod_block(l, b, n, bank):
                if n >= 1:
                    pe.wait_ge(mod_ready, n)
                for q in range(2):
                    item = ("mod", l, b, q)
                    arrived(pe, item)
                    w = ring[:, slot(item), :].rearrange("p (k n) -> p k n", k=4)
                    for k in range(4):
                        for half in range(2):
                            g = 2 * (k % 2) + half
                            mm = matmul(PS[32 * g:32 * g + 32, bank, :], cpad[:, 4 * q + k, 2 - 2 * l:34 - 2 * l],
                                        w[:, k, BANK * half:BANK * half + BANK],
                                        start=(q == 0 and k < 2), stop=(q == 1 and k >= 2))
                    mm.then_inc(used, 1)

            def broadcast(bank, l, b):
                for s in range(S):
                    for half in range(2):
                        mm = matmul(PS[:, bank[s] + half, :], selb_c[:, l, s, half, :], modrow[:, b, :], True, True)
                return mm

            def keep_warm(k, bank):
                for _ in range(k):
                    matmul(PS[:, bank, :], ident, const[:, 0:BANK], True, True)

            def shifts(n, l, b):
                for s in range(S):
                    if s:
                        pe.wait_ge(x_ready, 2 * n - 1)
                    for half in range(2):
                        mm = matmul(PS[:, 4 + 2 * s + half, :], selb_c[:, l, s, half, :], modrow[:, b, :], True, True)
                    mm.then_inc(shift_done, 1)
                pe.wait_ge(x_ready, 2 * n)
                keep_warm(2, 1)

            def turn_stream(n, s):
                pe.wait_ge(h_ready, 2 * n + s + 1)
                for k in range(KT):
                    mm = nc.tensor.transpose(PS[:, 2 * s + k // 4, P * (k % 4):P * (k % 4) + P],
                                             H[:, s, k, :], ident)
                mm.then_inc(ht_done, 1)

            def turn_h(n):
                for s in range(S):
                    turn_stream(n, s)

            def logits(l, s):
                if s == 0:
                    pe.wait_ge(router_in, 32 * (l + 1))
                    pe.wait_ge(late_params_in, 16 * 12)
                for k in range(KT):
                    matmul(PS[0:NG + NE, 4, P * s:P * s + P], RW[:, k, :], HT[:, k, P * s:P * s + P], k == 0, False)
                return matmul(PS[0:NG + NE, 4, P * s:P * s + P], rbias[:, l, :], cst("ones")[0:1, :], False, True)

            pe.wait_ge(params_in, 64)
            nc.tensor.transpose(PS[:, 1, 0:24], lbrow[:, :], ident[0:24, 0:24]).then_inc(lb_turned, 1)
            pe.wait_ge(start_dve, 1)
            pe.wait_ge(pad_clear, 3)
            mod_block(0, 1, 0, 6)
            keep_warm(2, 4)
            pe.wait_ge(lb_ready, 1)
            pe.wait_ge(mod_ready, 1)
            broadcast((0, 2), 0, 1).then_inc(scale_done, 1)
            keep_warm(3, 4)
            mod_block(0, 0, 1, 6)
            pe.wait_ge(mod_ready, 2)
            broadcast((4, 6), 0, 0).then_inc(shift_done, 1)
            turn_h(0)

            pe.wait_ge(ht_ready_a, 2)
            pe.wait_ge(ht_ready_v, 2)
            late = list(MOD_LATE)

            def late_mod(bank):
                l, b = late.pop(0)
                mod_block(l, b, 2 + len(MOD_LATE) - len(late) - 1, bank)

            for i, c in enumerate(EVEN_ORDER[:4]):
                item = ("even_in", c)
                bank = 2 * i
                if i == 3:
                    pe.wait_ge(mod_ready, 4)
                arrived(pe, item)
                w = ring[:, slot(item), :].rearrange("p (k n) -> p k n", k=KT)
                if c in (QA, ZF, ZB):
                    for h in range(HA):
                        for k in range(KT):
                            mm = matmul(PS[:, bank + h // 2, 256 * (h % 2):256 * (h % 2) + 256],
                                        w[:, k, P * h:P * h + P], HT[:, k, :], k == 0, k == KT - 1)
                else:
                    for s in range(S):
                        for k in range(KT):
                            mm = matmul(PS[:, bank + s, :], HT[:, k, P * s:P * s + P], w[:, k, :],
                                        k == 0, k == KT - 1)
                mm.then_inc(used, 1)
                if i in MOD_BANK:
                    if i == 3:
                        pe.wait_ge(in_free_a, 2)
                    late_mod(MOD_BANK[i])

            halves = [(c, s) for c in EVEN_ORDER[4:] for s in range(S)]

            def half_chunk():
                n = 6 - len(halves)
                c, s = halves.pop(0)
                item = ("even_in", c)
                if n:
                    pe.wait_ge(half_read, n)
                arrived(pe, item)
                w = ring[:, slot(item), :].rearrange("p (k n) -> p k n", k=KT)
                for k in range(KT):
                    mm = matmul(PS[:, 7, :], HT[:, k, P * s:P * s + P], w[:, k, :], k == 0, k == KT - 1)
                mm.then_inc(used if s else half_done, 1)

            for g in range(4):
                s, d = g // 2, g % 2
                pe.wait_ge(lf_ready, d + 1)
                if g:
                    pe.wait_ge(masked_ready, g)
                else:
                    pe.wait_ge(in_free_v, 2)
                for h in range(HA):
                    mm = nc.tensor.transpose(PS[:, 4, P * h:P * h + P], LF[:, d, h, P * s:P * s + P], ident)
                mm.then_inc(lft_done, 1)
                if g >= 2:
                    pe.wait_ge(decayed_ready, g)
                    late_mod(5)
                else:
                    half_chunk()
                pe.wait_ge(lft_ready, g + 1)
                if g:
                    pe.wait_ge(states_ready, g)
                else:
                    pe.wait_ge(mod_ready, 5)
                for h in range(HA):
                    mm = matmul(PS[:, h, 0:3 * P], LFT[:, h, :], cums_c[:, d, :], True, True)
                mm.then_inc(cums_done, 1)
                if g < 2:
                    half_chunk()
                else:
                    pe.wait_ge(mod_ready, 2 * g + 4)
                    keep_warm(5, 5)
                pe.wait_ge(qk_ready, 4 * (g + 1))
                for h in range(HA):
                    mm = matmul(PS[:, 4, P * h:P * h + P], E1N[:, h, :], E1[:, h, :], True, True)
                mm.then_inc(scores_done, 1)
                if g < 2:
                    pe.wait_ge(in_free_v, 2)
                for h in range(HA):
                    mm = nc.tensor.transpose(PS[:, 5, P * h:P * h + P], E23[:, h, P:2 * P], ident)
                mm.then_inc(decayed_turned, 1)
                if g == 0:
                    half_chunk()
                elif g == 1:
                    pe.wait_ge(half_read, 6)
                    late_mod(7)
                pe.wait_ge(decayed_ready, g + 1)
                if g == 0:
                    pe.wait_ge(in_free_a, 3)
                for h in range(HA):
                    for n in range(NSUB):
                        mm = matmul(PS[:, n, P * h:P * h + P], K2[SUB * n:SUB * n + SUB, h, :],
                                    IV[SUB * n:SUB * n + SUB, s, P * h:P * h + P], True, True)
                mm.then_inc(kv_done, 1)
                if g == 0:
                    half_chunk()
                elif g == 1:
                    late_mod(7)
                else:
                    late_mod(5)
                pe.wait_ge(masked_ready, g + 1)
                if g == 2:
                    pe.wait_ge(mod_ready, 7)
                for h in range(HA):
                    matmul(PS[:, 6 + s, P * h:P * h + P], LFT[:, h, :], IV[:, s, P * h:P * h + P],
                           d == 0 and h == 0, False)
                pe.wait_ge(states_ready, g + 1)
                order = list(range(NSUB)) if d == 0 else list(range(NSUB))[::-1]
                for h in range(HA):
                    for i, n in enumerate(order):
                        if i == 0 and s == 0:
                            continue
                        start_state = S0A[:, d, P * h:P * h + P] if i == 0 else ST[:, i - 1, P * h:P * h + P]
                        mm = matmul(PS[SUB * n:SUB * n + SUB, 6 + s, P * h:P * h + P],
                                    E23[:, h, SUB * n:SUB * n + SUB], start_state, False, True)
                mm.then_inc(group_done, 1)
            def turn_hgrn(s):
                pe.wait_ge(hgrn_ready, s + 1)
                for h in range(HA):
                    mm = nc.tensor.transpose(PS[:, 4, P * h:P * h + P], GS[:, s, P * h:P * h + P], ident)
                mm.then_inc(hgrn_turned, 1)

            def turn_qk(s):
                pe.wait_ge(attn_qk_ready, s + 1)
                for j in range(6):
                    mm = nc.tensor.transpose(PS[:, 2 * s + j // 4, P * (j % 4):P * (j % 4) + P], QKV[:, s, j, :], ident)
                if s:
                    for j in range(KVH):
                        mm = nc.tensor.transpose(PS[:, 3, P * (2 + j):P * (3 + j)], CKV[:, 0, P * j:P * j + P], ident)
                mm.then_inc(attn_qk_turned, 1)

            turn_hgrn(0)
            turn_qk(0)
            late_mod(5)
            turn_qk(1)
            for s in range(S):
                nk = 1 + s
                pe.wait_ge(attn_qkt_ready, s + 1)
                for h in range(HB):
                    for t in range(nk):
                        at = (h * nk + t) * P
                        mm = matmul(PS[:, 2 * s + at // BANK, at % BANK:at % BANK + P], AT_[s][:, h, :],
                                    AT_[s][:, 4 + 2 * t + h // 2, :], True, True)
                mm.then_inc(attn_scores_done, 1)
            pe.wait_ge(mix_ready, 1)
            turn_hgrn(1)
            for s in range(S):
                nk = 1 + s
                pe.wait_ge(attn_probs_ready, s + 1)
                for j in range(HB * nk):
                    mm = nc.tensor.transpose(PS[:, (6 if s else 1) + j // 4, P * (j % 4):P * (j % 4) + P],
                                             PR[s][:, j // nk, P * (j % nk):P * (j % nk) + P], ident)
                mm.then_inc(attn_probs_turned, 1)
            for s in range(S):
                nk = 1 + s
                pe.wait_ge(attn_probst_ready, s + 1)
                for h in range(HB):
                    for t in range(nk):
                        kv = h // 2
                        v = QKV[:, s, 6 + kv, :] if t == 0 else CKV[:, 1, P * kv:P * kv + P]
                        mm = matmul(PS[:, 2 * s, P * h:P * h + P], v, PRT[s][:, h * nk + t, :], t == 0, t == nk - 1)
                mm.then_inc(attn_out_done, 1)
            assert not late

            def project_out(kind, chunks, src, n):
                l = n // 2
                broadcast((4, 6), l, 2).then_inc(gate_done, 1)
                for q in range(chunks):
                    if q == 1:
                        pe.wait_ge(gate_ready, n + 2)
                        broadcast((4, 6), l, 4).then_inc(scale_done, 1)
                    item = (kind, q)
                    arrived(pe, item)
                    w = ring[:, slot(item), :].rearrange("p (k n) -> p k n", k=4)
                    for k in range(4):
                        kk = 4 * q + k
                        for s in range(S):
                            for half in range(2):
                                mm = matmul(PS[:, 2 * s + half, :], src[:, kk, P * s:P * s + P],
                                            w[:, k, BANK * half:BANK * half + BANK],
                                            kk == 0, kk == 4 * chunks - 1)
                    mm.then_inc(used, 1)
                pe.wait_ge(scale_ready, 4 * l + 4)
                shifts(n + 1, l, 3)
                turn_h(n + 1)

            pe.wait_ge(mix_ready, 4)
            pe.wait_ge(mod_ready, 2 + len(MOD_LATE))
            project_out("even_out", 2, HT, 0)

            def moe(l):
                base = AT[("moe", l, 0, 0)]
                ov = OV[l]
                pe.wait_ge(ht_ready_a, 4 * l + 3)
                pe.wait_ge(ht_ready_v, 4 * l + 3)
                logits(l, 0)
                pe.wait_ge(ht_ready_a, 4 * l + 4)
                pe.wait_ge(ht_ready_v, 4 * l + 4)
                logits(l, 1).then_inc(logit_sum, 1)
                pe.wait_ge(logit_read, l + 1)
                for s in range(S):
                    mm = nc.tensor.transpose(PS[:, 5, 256 + 64 * s:256 + 64 * s + NG + NE], LTS[:, P * s:P * s + P],
                                             ident[0:NG + NE, 0:NG + NE])
                mm.then_inc(logit_done, 1)

                prep = [(l, 5, s) for s in range(S)] + ([(1, 1, s) for s in range(S)] if l == 0 else [])

                def prepare(i):
                    l_, b, s = prep[i]
                    for half in range(2):
                        mm = matmul(PS[:, PREP_BANK[i] + half, :], selb_c[:, l_, s, half, :], modrow[:, b, :],
                                    True, True)
                    mm.then_inc(prep_done, 1)

                def start_zero(a):
                    if a + 1 < len(prep):
                        pe.wait_ge(prep_read, 4 * l + a + 2)
                    for half in range(2):
                        matmul(PS[:, 2 * a + half, :], zero, const[0:1, 0:BANK], True, False)

                for i in range(min(3, len(prep))):
                    prepare(i)
                pe.wait_ge(mask_ready, l + 1)
                matmul(PS[:, 5, 0:NE], cst("upper"), MASK[:, 0, :], True, True)
                matmul(PS[:, 5, 64:64 + NE], cst("ones"), MASK[:, 0, :], True, False)
                matmul(PS[:, 5, 64:64 + NE], cst("upper"), MASK[:, 1, :], False, True)
                matmul(PS[:, 5, 128:128 + NE], cst("ones"), MASK[:, 0, :], True, False)
                matmul(PS[:, 5, 128:128 + NE], cst("ones"), MASK[:, 1, :], False, True).then_inc(prefix_done, 1)
                start_zero(0)
                if len(prep) > 3:
                    prepare(3)

                def gather(half, par):
                    for k in range(4):
                        for s in range(S):
                            mm = matmul(PS[:, 4 + half, P * k:P * k + P], H[:, s, 4 * half + k, :],
                                        SEL[:, par, s, :], s == 0, s == S - 1)
                    return mm

                def turn_select(par):
                    for s in range(S):
                        mm = nc.tensor.transpose(PS[:, 7, 256 + P * s:256 + P * s + P], WSEL[:, par, s, :], ident)
                    return mm

                def turn_act():
                    for j in range(2):
                        mm = nc.tensor.transpose(PS[:, 7, P * j:P * j + P], ACTB[:, P * j:P * j + P], ident)
                    return mm

                def gate_or_up(m, slot_, par):
                    w = ring[:, slot_, :].rearrange("p (e k f) -> p e k f", e=2, k=KT)
                    for k in range(KT):
                        for e in range(2):
                            mm = matmul(PS[CAP * e:CAP * e + CAP, 6, FE * m:FE * m + FE],
                                        XG[:, par, k, CAP * e:CAP * e + CAP], w[:, e, k, :], k == 0, k == KT - 1)
                    return mm

                def down(half, slot_):
                    w = ring[:, slot_, :].rearrange("p (e j n) -> p e j n", e=2, j=2)
                    for j in range(2):
                        for e in range(2):
                            mm = matmul(PS[CAP * e:CAP * e + CAP, 4 + half, :], ACTT[:, j, CAP * e:CAP * e + CAP],
                                        w[:, e, j, BANK * half:BANK * half + BANK], j == 0, j == 1)
                    return mm

                def scatter(par):
                    for s in range(S):
                        for half in range(2):
                            mm = matmul(PS[:, 2 * s + half, :], WSELT[:, par, s, :], YG[:, half, :], False, False)
                    return mm

                def pair(p, par, first=False, last=False):
                    t = p + 16 * l
                    lap = (base + 3 * par) // RING
                    sl = [(base + 3 * par + m) % RING for m in range(3)]
                    lv = [16 * ((base + 3 * par + m) // RING + 1) for m in range(3)]
                    p2 = (p - par) * 8
                    pe.wait_ge(xg0_ready, t + 1)
                    pe.wait_ge(xg1_ready, t + 1)
                    if not (first and l == 0):
                        pe.wait_ge(act_ready, t)
                    pe.wait_ge(landed[sl[0]], p2 + lv[0])
                    gate_or_up(0, sl[0], par).then_inc(used, 1)
                    if first:
                        start_zero(1)
                    else:
                        pe.wait_ge(yg0_ready, t)
                        pe.wait_ge(yg1_ready, t)
                        pe.wait_ge(wselt_ready, t)
                        scatter(1 - par)
                    pe.wait_ge(landed[sl[1]], p2 + lv[1])
                    gate_or_up(1, sl[1], par).then_inc(used, 1)
                    if not last:
                        pe.wait_ge(sel_ready, p * 2 + (34 * l + 4))
                        gather(0, 1 - par).then_inc(gather0_done, 1)
                        pe.wait_ge(wsel_ready, p * 2 + (34 * l + 4))
                        pe.wait_ge(wselt_ready, t + 1)
                        turn_select(1 - par)
                    pe.wait_ge(act_ready, t + 1)
                    turn_act().then_inc(turn_done, 1)
                    if not last:
                        gather(1, 1 - par).then_inc(gather1_done, 1)
                        pe.wait_ge(xg0_ready, t + 2)
                    pe.wait_ge(actt_ready, t + 1)
                    pe.wait_ge(landed[sl[2]], p2 + lv[2])
                    down(0, sl[2]).then_inc(down0_done, 1)
                    if not last:
                        pe.wait_ge(xg1_ready, t + 2)
                    down(1, sl[2]).then_inc(used, 1)

                pe.wait_ge(sel_ready, 34 * l + 2)
                gather(0, 0).then_inc(gather0_done, 1)
                gather(1, 0).then_inc(gather1_done, 1)
                pe.wait_ge(prep_read, 4 * l + len(prep))
                pe.wait_ge(wsel_ready, 34 * l + 2)
                turn_select(0).then_inc(turn_done, 1)
                pair(0, 0, first=True)
                with pe.Fori(0, NPAIR // 2 - 1) as i:
                    pair(i * 2 + 1, 1)
                    pair(i * 2 + 2, 0)
                pair(NPAIR - 1, 1, last=True)
                pe.wait_ge(yg0_ready, 16 * l + NPAIR)
                pe.wait_ge(yg1_ready, 16 * l + NPAIR)
                pe.wait_ge(wselt_ready, 16 * l + NPAIR)
                scatter(1)

                pe.wait_ge(count_ready, l + 1)
                most = pe.value_load(CNT[0:1, 0:1], min_val=0, max_val=S * P)
                with pe.If(most > CAP):
                    matmul(PS[:, 0, :], zero, const[0:1, 0:BANK], False, False).then_inc(ov["used"], 1)
                    matmul(PS[:, 1, :], zero, const[0:1, 0:BANK], False, False).then_inc(ov["scat"], 1)
                    with pe.Fori(0, ROUNDS - 1) as r:
                        with pe.Fori(0, NPAIR) as p:
                            t = r * NPAIR + p
                            pe.wait_ge(ov["sel"], t * 4 + 4)
                            pe.wait_ge(ov["yg"], t * 2 + 1)
                            gather(0, 0)
                            gather(1, 0)
                            turn_select(0).then_inc(ov["gath"], 1)
                            pe.wait_ge(ov["xg"], t * 3 + 3)
                            pe.wait_ge(ov["in0"], t * 16 + 16)
                            gate_or_up(0, 0, 0).then_inc(ov["used"], 1)
                            pe.wait_ge(ov["in1"], t * 16 + 16)
                            gate_or_up(1, 1, 0).then_inc(ov["used"], 1)
                            pe.wait_ge(ov["act"], t + 1)
                            turn_act().then_inc(ov["turn"], 1)
                            pe.wait_ge(ov["actt"], t + 1)
                            pe.wait_ge(ov["in2"], t * 16 + 16)
                            down(0, 2)
                            down(1, 2).then_inc(ov["used"], 1)
                            pe.wait_ge(ov["yg"], t * 2 + 3)
                            scatter(0).then_inc(ov["scat"], 1)
                matmul(PS[:, 3, 0:SUB], zero, const[0:1, 0:SUB], False, True).then_inc(branch_done, 1)

            moe(0)
            shifts(2, 1, 0)
            turn_stream(2, 0)

            def odd_part(c, s, tiles):
                w = ring[:, slot(("odd_in", c)), :].rearrange("p (k n) -> p k n", k=KT)
                for k in tiles:
                    mm = matmul(PS[:, 2 * (c % 4) + s, :], HT[:, k, P * s:P * s + P], w[:, k, :], k == 0, k == KT - 1)
                return mm

            pe.wait_ge(ht_ready_a, 5)
            pe.wait_ge(ht_ready_v, 5)
            arrived(pe, ("odd_in", 0))
            odd_part(0, 0, range(2))
            turn_stream(2, 1)
            odd_part(0, 0, range(2, KT))
            pe.wait_ge(ht_ready_a, 6)
            pe.wait_ge(ht_ready_v, 6)
            odd_part(0, 1, range(KT)).then_inc(used, 1)
            for c in range(1, 5):
                if c == 4:
                    pe.wait_ge(odd_free_a, 1)
                    pe.wait_ge(odd_free_v, 1)
                arrived(pe, ("odd_in", c))
                odd_part(c, 0, range(KT))
                odd_part(c, 1, range(KT)).then_inc(used, 1)
            pe.wait_ge(odd_free_a, 5)
            pe.wait_ge(odd_free_v, 5)
            pe.wait_ge(decay_ready, HC)
            pe.wait_ge(ret_keys_scaled, 1)

            def odd_half(c, s):
                n = ODD_HALVES.index((c, s))
                if n:
                    pe.wait_ge(odd_half_read, n)
                arrived(pe, ("odd_in", c))
                w = ring[:, slot(("odd_in", c)), :].rearrange("p (k n) -> p k n", k=KT)
                for k in range(KT):
                    mm = matmul(PS[:, 3, :], HT[:, k, P * s:P * s + P], w[:, k, :], k == 0, k == KT - 1)
                if s:
                    mm.then_inc(used, 3 if c == 11 else 1)
                else:
                    mm.then_inc(odd_half_done, 1)

            for s in range(S):
                for h in range(HC):
                    u = HC * s + h
                    if u == HC:
                        pe.wait_ge(ret_rope_done, 1)
                        arrived(pe, ("state", 0))
                        arrived(pe, ("state", 1))
                    if u:
                        pe.wait_ge(ret_qkt_ready, u)
                    for j in range(4):
                        at = 1024 * (j // 2) + 256 * h + P * (j % 2)
                        mm = nc.tensor.transpose(PS[:, 0, P * j:P * j + P], QKc[:, s, at:at + P], ident)
                    mm.then_inc(ret_qk_turned, 1)
                    odd_half(*HEAD_HALVES[u][0])
                    pe.wait_ge(ret_qkt_ready, u + 1)
                    for j in range(2):
                        mm = matmul(PS[:, 1, 0:P], TT[:, 2 + j, :], TT[:, j, :], j == 0, j == 1)
                    mm.then_inc(ret_scores_done, 1)
                    if s == 0:
                        pe.wait_ge(ret_kd_ready, 2 * (h + 1))
                        for d in range(2):
                            for j in range(2):
                                n = 4 * h + 2 * d + j
                                if n >= 4:
                                    pe.wait_ge(ret_state_ready, n - 3)
                                matmul(PS[:, 4 + n % 4, :], KD[:, d, P * j:P * j + P],
                                       VY[:, 0, VC * h:VC * h + VC], True, True).then_inc(ret_state_done, 1)
                    if len(HEAD_HALVES[u]) == 2:
                        odd_half(*HEAD_HALVES[u][1])
                    pe.wait_ge(ret_masked_ready, u + 1)
                    if u:
                        pe.wait_ge(ret_y_ready, u)
                    mm = matmul(PS[:, 2, :], PC, VY[:, s, VC * h:VC * h + VC], True, s == 0)
                    if s:
                        pe.wait_ge(ret_qd_ready, h + 1)
                        for d in range(2):
                            st = ring[:, slot(("state", d)), :].rearrange("p (h j v) -> p h j v", h=HC, j=2)
                            for j in range(2):
                                mm = matmul(PS[:, 2, :], QD[:, 2 * d + j, :], st[:, h, j, :], False, d == 1 and j == 1)
                    mm.then_inc(ret_out_done, 1)
            odd_half(*ODD_HALVES[-1])
            for s in range(S):
                for q in range(4):
                    u = 4 * s + q
                    pe.wait_ge(gated_ready, u + 1)
                    if u >= 2:
                        pe.wait_ge(odd_mix_ready, u - 1)
                    for j in range(4):
                        mm = nc.tensor.transpose(PS[:, u % 2, P * j:P * j + P],
                                                 VY[:, s, BANK * q + P * j:BANK * q + P * j + P], ident)
                    mm.then_inc(gated_turned, 1)
            pe.wait_ge(odd_mix_ready, 8)
            pe.wait_ge(ret_y_ready, 2 * HC)
            pe.wait_ge(odd_half_read, len(ODD_HALVES))
            pe.wait_ge(ret_state_ready, 16)
            project_out("odd_out", 4, MIXC, 2)
            moe(1)

        @block.scalar
        def _(act):
            st = Steps(act, a_step)
            A_ = nc.scalar.activation

            def norm(n):
                for s in range(S):
                    if n:
                        act.wait_ge(x_ready, 2 * n + s - 1)
                    else:
                        act.wait_ge(x_in, 32)
                    A_(squares[:, s, :], X[:, s, :], SQUARE, accum_out=sumsq[:, s:s + 1]).then_inc(sq_ready, 1)
                    act.wait_ge(sq_ready, 2 * n + s + 1)
                    A_(sumsq[:, s:s + 1], sumsq[:, s:s + 1], SQRT, scale=1.0 / D, bias=EPS_COL).then_inc(std_ready, 1)

            def evac_ht(n):
                for s in range(S):
                    act.wait_ge(ht_done, 2 * n + s + 1)
                    A_(HT[:, 0:4, P * s:P * s + P], PS[:, 2 * s, :].rearrange("p (k t) -> p k t", k=4), COPY)\
                        .then_inc(ht_ready_a, 1)

            def gates(n):
                act.wait_ge(gate_done, n // 2 + 1)
                for s in range(S):
                    A_(GATE[:, s, :], PS[:, 4 + 2 * s:6 + 2 * s, :].rearrange("p b n -> p (b n)"), COPY)\
                        .then_inc(gate_ready, 1)

            EPS_COL = small[:, 150:151]
            act.wait_ge(params_in, 64)
            act.wait_ge(pad_clear, 3)
            A_(csig, cvec[:, :, :], SIGMOID).then_inc(start_act, 1)
            act.wait_ge(start_dve, 2)
            A_(lbtmp[:, :, :], lbtmp[:, :, :], EXP).then_inc(start_act, 1)
            norm(0)
            act.wait_ge(params_in, 80)
            evac_ht(0)

            for i, c in enumerate(EVEN_ORDER[:4]):
                bank = 2 * i
                byhead = PS[:, bank:bank + 2, :].rearrange("p b n -> p (b n)").rearrange("p (h t) -> p h t", h=HA)
                act.wait_ge(used, AT[("even_in", c)] + 1)
                if c in (ZF, ZB):
                    d = 0 if c == ZF else 1
                    A_(LF[:, d, :, :], byhead, SIGMOID).then_inc(f_ready, 1)
                    A_(KEYT[:, d, :, :], byhead, SIGMOID, scale=-1.0).then_inc(in_free_a, 1)
                elif c == QA:
                    A_(SG[:, :, :], byhead, SIGMOID).then_inc(f_ready, 1)
                    for d in range(2):
                        act.wait_ge(key_ready, 2 * d + 1)
                        A_(LF[:, d, :, :], LF[:, d, :, :], LN).then_inc(lf_ready, 1)
                else:
                    A_(IV[:, 0, :], PS[:, bank, :], COPY).then_inc(in_free_a, 1)

            def first_half(c):
                act.wait_ge(half_done, EVEN_ORDER.index(c) - 3)
                if c == GA:
                    A_(GS[:, 0, :], PS[:, 7, :], SILU).then_inc(half_read, 1)
                else:
                    A_(QKV[:, 0, (0 if c == QB else 4):(4 if c == QB else 8), :],
                       PS[:, 7, :].rearrange("p (a b) -> p a b", a=4), COPY).then_inc(half_read, 1)

            def hgrn_norm(s, junk):
                for h in range(HA):
                    st.link(A_(junk, PS[:, 6 + s, P * h:P * h + P], SQUARE,
                               accum_out=ssA[:, HA * s + h:HA * s + h + 1]))
                A_(ssA[:, HA * s:HA * s + HA], ssA[:, HA * s:HA * s + HA], SQRT, scale=1.0 / P, bias=EPS_COL)\
                    .then_inc(hgrn_std, 1)

            for g in range(4):
                if g == 0:
                    first_half(QB)
                elif g == 1:
                    first_half(GA)
                act.wait_ge(cums_done, g + 1)
                if g:
                    act.wait_ge(group_done, g)
                A_(E1[:, :, :], PS[:, 0:4, 0:P], EXP).then_inc(exps_ready, 1)
                A_(E1N[:, :, :], PS[:, 0:4, 0:P], EXP, scale=-1.0).then_inc(exps_ready, 1)
                A_(E23[:, :, :], PS[:, 0:4, P:3 * P], EXP).then_inc(exps_ready, 1)
                if g == 1:
                    act.wait_ge(used, AT[("even_in", GA)] + 1)
                    A_(GS[:, 1, :], PS[:, 7, :], SILU).then_inc(half_read, 1)
                act.wait_ge(decayed_turned, g + 1)
                A_(K2[:, :, :], PS[:, 5, :].rearrange("p (h k) -> p h k", h=HA), COPY).then_inc(decayed_ready, 1)
                if g == 0:
                    first_half(KVB)
                elif g == 2:
                    hgrn_norm(0, LFV[:, 6, :])
                    act.wait_ge(attn_sq, 2)
                    A_(ssB, ssB, SQRT, scale=1.0 / P, bias=EPS_COL).then_inc(attn_std, 1)
            def evac_qk(s):
                act.wait_ge(attn_qk_turned, s + 1)
                A_(AT_[s].rearrange("p a b -> p (a b)"),
                   PS[:, 2 * s:2 * s + 2, :].rearrange("p b n -> p (b n)")[:, 0:P * (6 + 2 * s)], COPY)\
                    .then_inc(attn_qkt_ready, 1)

            def evac_hgrn(s):
                act.wait_ge(hgrn_turned, s + 1)
                A_(HT[:, 0:4, P * s:P * s + P], PS[:, 4, :].rearrange("p (k t) -> p k t", k=4), COPY)\
                    .then_inc(mix_ready, 1)

            def exps(s):
                nk = 1 + s
                act.wait_ge(attn_max_ready, s + 1)
                for h in range(HB):
                    src = PS[:, 2 * s:2 * s + 2, :].rearrange("p b n -> p (b n)")[:, P * nk * h:P * nk * (h + 1)]
                    A_(PR[s][:, h, :], src, EXP, scale=float(P) ** -0.5, bias=nbB[s][:, h:h + 1],
                       accum_out=smB[s][:, h:h + 1]).then_inc(attn_exp_ready, 1)

            act.wait_ge(group_done, 4)
            evac_qk(0)
            hgrn_norm(1, E1[:, 0, :])
            evac_hgrn(0)
            evac_qk(1)
            exps(0)
            evac_hgrn(1)
            exps(1)
            for s in range(S):
                act.wait_ge(attn_probs_turned, s + 1)
                b = 6 if s else 1
                A_(PRT[s].rearrange("p a b -> p (a b)"),
                   PS[:, b:b + 1 + s, :].rearrange("p b n -> p (b n)"), COPY).then_inc(attn_probst_ready, 1)
            for s in range(S):
                act.wait_ge(attn_out_done, s + 1)
                A_(HT[:, 4:8, P * s:P * s + P], PS[:, 2 * s, :].rearrange("p (k t) -> p k t", k=4), COPY)\
                    .then_inc(mix_ready, 1)
            act.wait_ge(state_out, 32)
            gates(0)

            def moe(l):
                ov = OV[l]

                def prep(i, dst):
                    act.wait_ge(prep_done, 4 * l + i + 1)
                    A_(dst, PS[:, PREP_BANK[i]:PREP_BANK[i] + 2, :].rearrange("p b n -> p (b n)"), COPY)\
                        .then_inc(prep_read, 1)

                act.wait_ge(group_diff, l + 1)
                A_(G4[:, 1, :], G4[:, 1, :], EXP).then_inc(group_exp, 1)
                prep(0, GATE[:, 0, :])
                prep(1, GATE[:, 1, :])
                act.wait_ge(expert_diff, l + 1)
                A_(s1[:, 8:10], s1[:, 8:10], EXP).then_inc(expert_exp, 1)
                if l == 0:
                    prep(2, GAIN[:, 0, :])
                    prep(3, GAIN[:, 1, :])

                def xg_half(half, par):
                    return A_(XG[:, par, 4 * half:4 * half + 4, :].rearrange("p k t -> p (k t)"), PS[:, 4 + half, :], COPY)

                def wselt(par):
                    return A_(WSELT[:, par, :, :].rearrange("p s t -> p (s t)"), PS[:, 7, 256:512], COPY)

                def pair(p, par, last=False):
                    t = p + 16 * l
                    act.wait_ge(used, p * 3 + (AT[("moe", l, 0, 0)] + 2))
                    A_(SILB, PS[:, 6, 0:FE], SILU).then_inc(silu_ready, 1)
                    if not last:
                        act.wait_ge(gather0_done, t + 2)
                        xg_half(0, 1 - par).then_inc(xg0_ready, 1)
                    act.wait_ge(turn_done, p + (17 * l + 2))
                    A_(ACTT[:, :, :].rearrange("p j t -> p (j t)"), PS[:, 7, 0:256], COPY).then_inc(actt_ready, 1)
                    if not last:
                        wselt(1 - par).then_inc(wselt_ready, 1)
                    act.wait_ge(used, p * 3 + (AT[("moe", l, 0, 0)] + 3))
                    A_(YG[:, 1, :], PS[:, 5, :], COPY).then_inc(yg1_ready, 1)

                act.wait_ge(gather0_done, 16 * l + 1)
                xg_half(0, 0).then_inc(xg0_ready, 1)
                act.wait_ge(turn_done, 17 * l + 1)
                wselt(0).then_inc(wselt_ready, 1)
                pair(0, 0)
                with act.Fori(0, NPAIR // 2 - 1) as i:
                    pair(i * 2 + 1, 1)
                    pair(i * 2 + 2, 0)
                pair(NPAIR - 1, 1, last=True)
                act.wait_ge(count_ready, l + 1)
                most = act.value_load(CNT[0:1, 0:1], min_val=0, max_val=S * P)
                with act.If(most > CAP):
                    A_(small[:, 152:153], EPS_COL, COPY).then_inc(ov["yg"], 1)
                    with act.Fori(0, ROUNDS - 1) as r:
                        with act.Fori(0, NPAIR) as p:
                            t = r * NPAIR + p
                            act.wait_ge(ov["gath"], t + 1)
                            xg_half(0, 0).then_inc(ov["xg"], 1)
                            xg_half(1, 0).then_inc(ov["xg"], 1)
                            wselt(0).then_inc(ov["xg"], 1)
                            act.wait_ge(ov["used"], t * 3 + 3)
                            A_(SILB, PS[:, 6, 0:FE], SILU).then_inc(ov["sil"], 1)
                            act.wait_ge(ov["turn"], t + 1)
                            A_(ACTT[:, :, :].rearrange("p j t -> p (j t)"), PS[:, 7, 0:256], COPY)\
                                .then_inc(ov["actt"], 1)
                            act.wait_ge(ov["used"], t * 3 + 4)
                            A_(YG[:, 0, :], PS[:, 4, :], COPY).then_inc(ov["yg"], 1)
                            A_(YG[:, 1, :], PS[:, 5, :], COPY).then_inc(ov["yg"], 1)
            norm(1)
            evac_ht(1)
            moe(0)
            norm(2)
            evac_ht(2)

            def evac_odd(c):
                bank = 2 * (c % 4)
                act.wait_ge(used, AT[("odd_in", c)] + 1)
                dst = QKc[:, 0, 512 * c:512 * c + 512] if c < 4 else VY[:, 0, 512 * (c - 4):512 * (c - 4) + 512]
                A_(dst, PS[:, bank, :], COPY).then_inc(odd_free_a, 1)

            act.wait_ge(late_params_in, 16 * 12)
            st.link(A_(LG, LG, SIGMOID))
            st.mark(A_(LG, LG, LN))
            evac_odd(0)
            evac_odd(1)
            st.wait()
            for d in range(2):
                for h in range(HC):
                    j = HC * d + h
                    st.mark(A_(KDC[:, j:j + 1], powers_c[:, 2 + d:3 + d], EXP, scale=LG[:, j:j + 1]))
            for h in range(HC):
                if h:
                    act.wait_ge(decay_ready, h)
                A_(LGP[:, 0, :], cst("relp"), EXP, scale=LG[:, h:h + 1]).then_inc(powers_ready, 1)
                A_(LGP[:, 1, :], cst("relm"), EXP, scale=LG[:, HC + h:HC + h + 1]).then_inc(powers_ready, 1)
            for c in range(2, 5):
                evac_odd(c)

            def read_half(c, s):
                n = ODD_HALVES.index((c, s))
                if s:
                    act.wait_ge(used, AT[("odd_in", c)] + 1)
                else:
                    act.wait_ge(odd_half_done, c - 4)
                if c < 8:
                    A_(VY[:, 0, VC * (c - 4):VC * (c - 3)], PS[:, 3, :], COPY).then_inc(odd_half_read, 1)
                else:
                    g = n - 6
                    if g:
                        act.wait_ge(gated_ready, g)
                    A_(GB, PS[:, 3, :], SILU).then_inc(odd_half_read, 1)

            act.wait_ge(decay_ready, HC)
            for s in range(S):
                for h in range(HC):
                    u = HC * s + h
                    act.wait_ge(ret_qk_turned, u + 1)
                    if u:
                        act.wait_ge(ret_out_done, u)
                    A_(TT[:, :, :].rearrange("p a b -> p (a b)"), PS[:, 0, :], COPY).then_inc(ret_qkt_ready, 1)
                    if s:
                        if h:
                            act.wait_ge(ret_qd_ready, h)
                        A_(LGP[:, 0, :], cst("rowf"), EXP, scale=LG[:, h:h + 1]).then_inc(powers_ready, 1)
                        A_(LGP[:, 1, :], cst("rowb"), EXP, scale=LG[:, HC + h:HC + h + 1]).then_inc(powers_ready, 1)
                    read_half(*HEAD_HALVES[u][0])
                    if s == 0:
                        for j in range(4):
                            n = 4 * h + j
                            act.wait_ge(ret_state_done, n + 1)
                            if n >= 4:
                                act.wait_ge(ret_state_out[n % 4], 16 * (n // 4))
                            A_(SF[:, n % 4, :], PS[:, 4 + n % 4, :], COPY).then_inc(ret_state_ready, 1)
                    if u in (3, 4):
                        read_half(*HEAD_HALVES[u][1])
                    act.wait_ge(ret_stats, 2 * u + 1)
                    A_(sdC[:, u:u + 1], mvC[:, u, 1:2], SQRT, bias=EPS_COL).then_inc(ret_stats, 1)
            read_half(*ODD_HALVES[-1])
            for u in range(8):
                s, q = u // 4, u % 4
                if u % 2 == 0:
                    act.wait_ge(gated_turned, u + 1)
                    A_(MIXC[:, 4 * q:4 * q + 4, P * s:P * s + P], PS[:, 0, :].rearrange("p (k t) -> p k t", k=4), COPY)\
                        .then_inc(odd_mix_ready, 1)
                else:
                    act.wait_ge(gated_turned, u + 1)
                    A_(MIXC[:, 4 * q:4 * q + 4, P * s:P * s + P], PS[:, 1, :].rearrange("p (k t) -> p k t", k=4), COPY)\
                        .then_inc(odd_mix_ready, 1)
            gates(2)
            norm(3)
            evac_ht(3)
            moe(1)
            norm(4)

        @block.vector
        def _(dve):
            V = nc.vector
            st = Steps(dve, v_step)

            def mod_rows(l, b, n, bank):
                dve.wait_ge(used, AT[("mod", l, b, 1)] + 1)
                V.tensor_tensor(modrow[:, b, :], PS[:, bank, :], modrow[:, b, :], ALU.add).then_inc(mod_ready, 1)

            def gain_now(n):
                if n:
                    dve.wait_ge(gain_in, 16 * n)
                else:
                    dve.wait_ge(first_gain_in, 16)

            def scaled_gain(n, banks):
                dve.wait_ge(scale_done, {0: 1, 1: 2, 3: 3}[n])
                gain_now(n)
                for s in range(S):
                    V.scalar_tensor_tensor(out=GAIN[:, s, :], scalar=1.0, in1=gain[:, :], op0=ALU.add, op1=ALU.mult,
                                           in0=PS[:, banks[s]:banks[s] + 2, :].rearrange("p b n -> p (b n)"))\
                        .then_inc(scale_ready, 1)
                dve.wait_ge(scale_ready, 2 * n + 2)
                V.tensor_copy(small[:, 151:152], small[:, 150:151]).then_inc(gain_used, 1)

            def normalize(n, s, gains):
                dve.wait_ge(std_ready, 2 * n + s + 1)
                st.link(V.reciprocal(rstd[:, s:s + 1], sumsq[:, s:s + 1]))
                ins = V.scalar_tensor_tensor(out=normed[:, s, :], in0=X[:, s, :], scalar=rstd[:, s:s + 1], in1=gains,
                                             op0=ALU.mult, op1=ALU.mult)
                if n == 4:
                    ins.then_inc(h_ready, 1)
                else:
                    st.link(ins)

            def shift(n, s):
                dve.wait_ge(shift_done, 2 * n + s if n else 1)
                V.tensor_tensor(H[:, s, :, :].rearrange("t k p -> t p k"),
                                normed[:, s, :].rearrange("t (p k) -> t p k", k=KT),
                                PS[:, 4 + 2 * s:6 + 2 * s, :].rearrange("t b n -> t (b n)")
                                .rearrange("t (p k) -> t p k", k=KT), ALU.add).then_inc(h_ready, 1)

            def norm(n):
                dve.wait_ge(scale_ready, 2 * n + 2)
                for s in range(S):
                    normalize(n, s, GAIN[:, s, :])
                    shift(n, s)

            def evac_ht(n):
                for s in range(S):
                    dve.wait_ge(ht_done, 2 * n + s + 1)
                    V.tensor_copy(HT[:, 4:8, P * s:P * s + P], PS[:, 2 * s + 1, :].rearrange("p (k t) -> p k t", k=4))\
                        .then_inc(ht_ready_v, 1)

            def residual(n):
                if n % 2:
                    dve.wait_ge(branch_done, n // 2 + 1)
                    dve.wait_ge(prep_read, 2 if n == 1 else 6)
                else:
                    dve.wait_ge(used, AT[("even_out", 1) if n == 0 else ("odd_out", 3)] + 1)
                    dve.wait_ge(gate_ready, n + 2)
                for s in range(S):
                    st.link(V.tensor_tensor(GATE[:, s, :], PS[:, 2 * s:2 * s + 2, :].rearrange("p b n -> p (b n)"),
                                            GATE[:, s, :], ALU.mult))
                    V.tensor_tensor(X[:, s, :], X[:, s, :], GATE[:, s, :], ALU.add).then_inc(x_ready, 1)

            V.memset(modrow[:, :, :].bitcast(mybir.dt.uint32), 0).then_inc(pad_clear, 1)
            V.memset(cpad[:, :, :], 0.0).then_inc(pad_clear, 1)
            V.memset(small[:, 150:151], EPS).then_inc(pad_clear, 1)
            dve.wait_ge(start_act, 1)
            dve.wait_ge(pad_clear, 3)
            V.tensor_tensor(cpad[:, :, 2:2 + S], cvec[:, :, :].rearrange("p s k -> p k s"),
                            csig.rearrange("p s k -> p k s"), ALU.mult).then_inc(start_dve, 1)
            dve.wait_ge(lb_turned, 1)
            st.link(V.tensor_copy(lbcol[:, :, :].rearrange("p a b -> p (a b)"), PS[:, 1, 0:24]))
            st.link(V.tensor_tensor(lb[:, 0, :], lbcol[:, 0, :], lbcol[:, 1, :], ALU.max))
            st.link(V.tensor_tensor(lb[:, 0, :], lb[:, 0, :], lbcol[:, 2, :], ALU.max))
            for a in range(3):
                ins = V.tensor_tensor(lbtmp[:, a, :], lbcol[:, a, :], lb[:, 0, :], ALU.subtract)
                if a < 2:
                    st.mark(ins)
            st.wait()
            ins.then_inc(start_dve, 1)
            dve.wait_ge(start_act, 2)
            st.link(V.tensor_tensor(lb[:, 1, :], lbtmp[:, 0, :], lbtmp[:, 1, :], ALU.add))
            st.link(V.tensor_tensor(lb[:, 1, :], lb[:, 1, :], lbtmp[:, 2, :], ALU.add))
            st.link(V.reciprocal(lb[:, 1, :], lb[:, 1, :]))
            st.link(V.tensor_tensor(lb[:, 0, :], lbtmp[:, 0, :], lb[:, 1, :], ALU.mult))
            V.tensor_scalar(lb[:, 1, :], lb[:, 0, :], -1.0, 1.0, ALU.mult, ALU.add).then_inc(lb_ready, 1)
            dve.wait_ge(bias_in, 16 * 8)
            mod_rows(0, 1, 0, 6)
            scaled_gain(0, (0, 2))
            for s in range(S):
                normalize(0, s, GAIN[:, s, :])
            mod_rows(0, 0, 1, 6)
            for s in range(S):
                shift(0, s)
            evac_ht(0)

            dve.wait_ge(lb_ready, 1)
            late = list(MOD_LATE)

            def late_mod(bank):
                l, b = late.pop(0)
                mod_rows(l, b, 2 + len(MOD_LATE) - len(late) - 1, bank)

            for i, c in enumerate(EVEN_ORDER[:4]):
                bank = 2 * i
                flat = PS[:, bank:bank + 2, :].rearrange("p b n -> p (b n)")
                byhead = flat.rearrange("p (h t) -> p h t", h=HA)
                dve.wait_ge(used, AT[("even_in", c)] + 1)
                if c in (ZF, ZB):
                    d = 0 if c == ZF else 1
                    dve.wait_ge(f_ready, d + 1)
                    for h in range(HA):
                        j = HA * d + h
                        ins = V.tensor_scalar(LF[:, d, h, :], LF[:, d, h, :], lb[:, 1, j:j + 1], lb[:, 0, j:j + 1],
                                              ALU.mult, ALU.add)
                        if h < HA - 1:
                            st.mark(ins)
                    ins.then_inc(key_ready, 1)
                    dve.wait_ge(in_free_a, i + 1)
                    for h in range(HA):
                        j = HA * d + h
                        ins = V.tensor_scalar(KEYT[:, d, h, :], KEYT[:, d, h, :], lb[:, 1, j:j + 1], None, ALU.mult)
                        if h < HA - 1:
                            st.mark(ins)
                    ins.then_inc(key_ready, 1)
                    st.wait()
                elif c == QA:
                    dve.wait_ge(f_ready, 3)
                    V.scalar_tensor_tensor(out=QT[:, :, :], in0=byhead, scalar=float(P) ** -0.5, in1=SG[:, :, :],
                                           op0=ALU.mult, op1=ALU.mult).then_inc(in_free_v, 1)
                else:
                    V.tensor_copy(IV[:, 1, :], PS[:, bank + 1, :]).then_inc(in_free_v, 1)
                if i in MOD_BANK:
                    late_mod(MOD_BANK[i])

            def second_half(c):
                a = 0 if c == QB else 4
                dve.wait_ge(used, AT[("even_in", c)] + 1)
                V.tensor_copy(QKV[:, 1, a:a + 4, :], PS[:, 7, :].rearrange("p (a b) -> p a b", a=4))\
                    .then_inc(half_read, 1)

            def norm_qk(s):
                qk = QKV[:, s, 0:6, :]
                st.link(V.tensor_tensor(qk, qk, bcast(rsB[:, 6 * s:6 * s + 6].unsqueeze(2), [P, 6, P]), ALU.mult))
                st.mark(V.tensor_tensor(QKV[:, s, 0:4, :], QKV[:, s, 0:4, :],
                                        bcast(QNG[:, 0, :].unsqueeze(1), [P, 4, P]), ALU.mult))
                st.link(V.tensor_tensor(QKV[:, s, 4:6, :], QKV[:, s, 4:6, :],
                                        bcast(QNG[:, 1, :].unsqueeze(1), [P, 2, P]), ALU.mult))

            def rope_qk(a, n):
                x1, x2 = (QKV[:, 1, a:a + n, c:c + 64].rearrange("p (b c) t -> p b c t", c=2) for c in (0, 64))
                c_, s_ = (bcast(cst(x).unsqueeze(1).unsqueeze(1), [P, n // 2, 2, 64]) for x in ("cosb", "sinb"))
                t = [LFV[:, 2 * i:2 * i + n // 2, :].rearrange("p b (c t) -> p b c t", c=2) for i in range(4)]
                st.mark(V.tensor_tensor(t[0], x1, c_, ALU.mult))
                st.mark(V.tensor_tensor(t[1], x2, s_, ALU.mult))
                st.mark(V.tensor_tensor(t[2], x2, c_, ALU.mult))
                st.link(V.tensor_tensor(t[3], x1, s_, ALU.mult))
                st.mark(V.tensor_tensor(x1, t[0], t[1], ALU.subtract))
                st.link(V.tensor_tensor(x2, t[2], t[3], ALU.add))

            def hgrn_out(s):
                dve.wait_ge(hgrn_std, s + 1)
                st.link(V.reciprocal(rsA[:, HA * s:HA * s + HA], ssA[:, HA * s:HA * s + HA]))
                for h in range(HA):
                    j = HA * s + h
                    gsv = GS[:, s, P * h:P * h + P]
                    ins = V.scalar_tensor_tensor(out=gsv, in0=PS[:, 6 + s, P * h:P * h + P], scalar=rsA[:, j:j + 1],
                                                 in1=gsv, op0=ALU.mult, op1=ALU.mult)
                    if h < HA - 1:
                        st.mark(ins)
                st.wait()
                ins.then_inc(hgrn_ready, 1)

            dve.wait_ge(in_free_v, 2)
            dve.wait_ge(key_ready, 4)
            for g in range(4):
                s, d = g // 2, g % 2
                ts = slice(P * s, P * s + P)
                dve.wait_ge(lft_done, g + 1)
                if g:
                    dve.wait_ge(group_done, g)
                V.tensor_copy(LFT[:, :, :].rearrange("p h k -> p (h k)"), PS[:, 4, :]).then_inc(lft_ready, 1)
                if g >= 2:
                    late_mod(5)
                if g == 2:
                    dve.wait_ge(half_read, 6)
                    dve.wait_ge(late_params_in, 16 * 12)
                    V.tensor_tensor(GS[:, :, :], GS[:, :, :], bcast(GNA.unsqueeze(1), [P, S, 512]), ALU.mult)\
                        .then_inc(gs_ready, 1)
                    dve.wait_ge(group_done, 2)
                    for s_ in range(S):
                        st.link(V.tensor_tensor(LFV[:, 0:6, :], QKV[:, s_, 0:6, :], QKV[:, s_, 0:6, :], ALU.mult))
                        V.tensor_reduce(ssB[:, 6 * s_:6 * s_ + 6], LFV[:, 0:6, :], AX, ALU.add).then_inc(attn_sq, 1)
                        dve.wait_ge(attn_sq, s_ + 1)
                if g == 3:
                    dve.wait_ge(attn_std, 1)
                    st.link(V.reciprocal(rsB, ssB))
                    norm_qk(0)
                    V.tensor_copy(small[:, 151:152], small[:, 150:151]).then_inc(attn_qk_ready, 1)
                dve.wait_ge(exps_ready, 3 * g + 3)
                last = SUB - 1 if d == 0 else 0
                st.link(V.tensor_copy(DEC, E23[:, :, last:P:SUB]))
                V.tensor_tensor(E1[:, :, :], E1[:, :, :], QT[:, :, ts], ALU.mult).then_inc(qk_ready, 1)
                V.tensor_tensor(E1N[:, :, :], E1N[:, :, :], KEYT[:, d, :, ts], ALU.mult).then_inc(qk_ready, 1)
                V.tensor_tensor(E23[:, :, 0:P], E23[:, :, 0:P], QT[:, :, ts], ALU.mult).then_inc(qk_ready, 1)
                V.tensor_tensor(E23[:, :, P:2 * P], E23[:, :, P:2 * P], KEYT[:, d, :, ts], ALU.mult)\
                    .then_inc(qk_ready, 1)
                if g == 0:
                    second_half(QB)
                dve.wait_ge(scores_done, g + 1)
                V.tensor_tensor(LFT[:, :, :], PS[:, 4, :].rearrange("p (h k) -> p h k", h=HA),
                                bcast(cums_c[:, d, P:2 * P].unsqueeze(1), [P, HA, P]), ALU.mult).then_inc(masked_ready, 1)
                if g == 1:
                    late_mod(7)
                if g == 3:
                    norm_qk(1)
                dve.wait_ge(kv_done, g + 1)
                if g:
                    dve.wait_ge(state_out, 16 * min(g, 2))
                dve.wait_ge(late_params_in, 16 * 12)
                order = list(range(NSUB)) if d == 0 else list(range(NSUB))[::-1]
                for i, n in enumerate(order):
                    if s == 1 and i == NSUB - 1:
                        break
                    new = ST[:, i, :]
                    if s == 0 and i == 0:
                        st.link(V.tensor_copy(new, PS[:, n, :]))
                        continue
                    old = S0A[:, d, :] if i == 0 else ST[:, i - 1, :]
                    st.link(V.tensor_tensor(new.rearrange("p (h v) -> p h v", h=HA),
                                            old.rearrange("p (h v) -> p h v", h=HA),
                                            bcast(DEC[:, :, n:n + 1], [P, HA, P]), ALU.mult))
                    st.link(V.tensor_tensor(new, new, PS[:, n, :], ALU.add))
                V.tensor_copy(small[:, 151:152], small[:, 150:151]).then_inc(states_ready, 1)
                if g == 0:
                    second_half(KVB)
                else:
                    late_mod(7 if g == 1 else 5)
                if g == 2:
                    hgrn_out(0)
            rope_qk(0, 4)
            rope_qk(4, 2)
            V.tensor_copy(small[:, 151:152], small[:, 150:151]).then_inc(attn_qk_ready, 1)
            hgrn_out(1)
            late_mod(5)
            for s in range(S):
                nk = 1 + s
                dve.wait_ge(attn_scores_done, s + 1)
                src = PS[:, 2 * s:2 * s + 2, :].rearrange("p b n -> p (b n)")[:, 0:HB * P * nk]\
                    .rearrange("p (h t) -> p h t", h=HB)
                st.link(V.tensor_reduce(mxB[s], src, AX, ALU.max))
                V.tensor_scalar(nbB[s], mxB[s], -(float(P) ** -0.5), None, ALU.mult).then_inc(attn_max_ready, 1)
            for s in range(S):
                nk = 1 + s
                dve.wait_ge(attn_exp_ready, HB * (s + 1))
                st.link(V.reciprocal(riB[s], smB[s]))
                V.tensor_tensor(PR[s], PR[s], bcast(riB[s].unsqueeze(2), [P, HB, P * nk]), ALU.mult)\
                    .then_inc(attn_probs_ready, 1)
            dve.wait_ge(state_out, 32)
            scaled_gain(1, (4, 6))
            residual(0)

            def moe(l):
                ov = OV[l]
                dve.wait_ge(out_sem, 32)
                dve.wait_ge(logit_sum, l + 1)
                V.tensor_copy(LTS, PS[0:NG + NE, 4, 0:S * P]).then_inc(logit_read, 1)
                dve.wait_ge(logit_done, l + 1)
                st.link(V.tensor_copy(LGT[:, :, :], PS[:, 5, 256:384].rearrange("p (s n) -> p s n", s=S)[:, :, 0:NG + NE]))
                lg4 = LGT[:, :, 0:NG]
                g4 = [G4[:, i, :].rearrange("p (s g) -> p s g", s=S) for i in range(3)]
                gmax, gsum, prob = s1[:, 0:2], s1[:, 2:4], s1[:, 4:6]
                st.link(V.tensor_reduce(gmax, lg4, AX, ALU.max))
                gm = bcast(gmax.unsqueeze(2), [P, S, NG])
                st.mark(V.tensor_tensor(g4[0], lg4, gm, ALU.is_equal))
                V.tensor_tensor(g4[1], lg4, gm, ALU.subtract).then_inc(group_diff, 1)
                st.wait()
                st.link(V.tensor_tensor(g4[0], g4[0], bcast(cst("tie4").unsqueeze(1), [P, S, NG]), ALU.mult))
                st.link(V.tensor_reduce(s1[:, 6:8], g4[0], AX, ALU.max))
                st.link(V.tensor_tensor(g4[0], g4[0], bcast(s1[:, 6:8].unsqueeze(2), [P, S, NG]), ALU.is_equal))
                dve.wait_ge(group_exp, l + 1)
                st.link(V.tensor_reduce(gsum, g4[1], AX, ALU.add))
                st.mark(V.reciprocal(prob, gsum))
                lge = LGT[:, :, NG:].rearrange("p s (g e) -> p s g e", g=NG)
                for s in range(S):
                    st.mark(V.tensor_tensor(PRD[:, NG * s:NG * s + NG, :], lge[:, s, :, :],
                                            bcast(g4[0][:, s, :].unsqueeze(2), [P, NG, EG]), ALU.mult))
                st.wait()
                e8 = [E8[:, i, :].rearrange("p (s e) -> p s e", s=S) for i in range(8)]
                for s in range(S):
                    st.mark(V.tensor_reduce(e8[0][:, s, :], PRD[:, NG * s:NG * s + NG, :].rearrange("p g e -> p e g"),
                                            AX, ALU.add))
                st.wait()
                tie = bcast(cst("tie8").unsqueeze(1), [P, S, EG])

                def top(logits, m, hot):
                    st.link(V.tensor_reduce(m, logits, AX, ALU.max))
                    st.link(V.tensor_tensor(hot, logits, bcast(m.unsqueeze(2), [P, S, EG]), ALU.is_equal))
                    st.link(V.tensor_tensor(hot, hot, tie, ALU.mult))
                    st.link(V.tensor_reduce(s1[:, 12:14], hot, AX, ALU.max))
                    st.link(V.tensor_tensor(hot, hot, bcast(s1[:, 12:14].unsqueeze(2), [P, S, EG]), ALU.is_equal))

                m1, m2 = s1[:, 14:16], s1[:, 16:18]
                top(e8[0], m1, e8[1])
                st.link(V.scalar_tensor_tensor(out=e8[2], in0=e8[1], scalar=-BIG, in1=e8[0],
                                               op0=ALU.mult, op1=ALU.add))
                top(e8[2], m2, e8[3])
                V.tensor_tensor(s1[:, 8:10], m2, m1, ALU.subtract).then_inc(expert_diff, 1)
                st.link(V.tensor_tensor(e8[6], e8[1], e8[3], ALU.add))
                for s in range(S):
                    st.mark(V.tensor_tensor(MASK[:, s, :].rearrange("p (g e) -> p g e", g=NG),
                                            bcast(g4[0][:, s, :].unsqueeze(2), [P, NG, EG]),
                                            bcast(e8[6][:, s, :].unsqueeze(1), [P, NG, EG]), ALU.mult))
                st.wait()
                V.tensor_copy(small[:, 151:152], small[:, 150:151]).then_inc(mask_ready, 1)
                dve.wait_ge(expert_exp, l + 1)
                w1, w2 = s1[:, 18:20], s1[:, 20:22]
                st.link(V.tensor_scalar(w1, s1[:, 8:10], 1.0, None, ALU.add))
                st.link(V.reciprocal(w1, w1))
                st.link(V.tensor_tensor(w1, w1, prob, ALU.mult))
                st.link(V.tensor_tensor(w2, w1, s1[:, 8:10], ALU.mult))
                st.mark(V.tensor_tensor(e8[4], e8[1], bcast(w1.unsqueeze(2), [P, S, EG]), ALU.mult))
                st.mark(V.tensor_tensor(e8[5], e8[3], bcast(w2.unsqueeze(2), [P, S, EG]), ALU.mult))
                st.wait()
                st.link(V.tensor_tensor(e8[4], e8[4], e8[5], ALU.add))
                st.mark(V.memset(CW[:, :, NE:], 0.0))
                st.mark(V.memset(POS[:, :, NE:], -1.0))
                for s in range(S):
                    gh = bcast(g4[0][:, s, :].unsqueeze(2), [P, NG, EG])
                    st.mark(V.tensor_tensor(CW[:, s, 0:NE].rearrange("p (g e) -> p g e", g=NG), gh,
                                            bcast(e8[4][:, s, :].unsqueeze(1), [P, NG, EG]), ALU.mult))
                st.wait()
                dve.wait_ge(prefix_done, l + 1)
                pre = PS[:, 5, 0:128].rearrange("p (s n) -> p s n", s=S)[:, :, 0:NE]
                pos = POS[:, :, 0:NE]
                st.link(V.tensor_scalar(pos, pre, 1.0, None, ALU.add))
                st.link(V.tensor_tensor(pos, pos, MASK[:, :, :], ALU.mult))
                st.link(V.tensor_scalar(pos, pos, -1.0, None, ALU.add))
                st.link(V.tensor_reduce(s1[:, 22:23], PS[:, 5, 128:128 + NE], AX, ALU.max))
                V.tensor_copy(CNT[:, 0:1], s1[:, 22:23]).then_inc(count_ready, 1)

                def build(p, par, sel_sig):
                    for s in range(S):
                        ins = V.tensor_tensor(
                            SEL[:, par, s, :].rearrange("p (e c) -> p e c", e=2),
                            bcast(cst("slots").unsqueeze(1), [P, 2, CAP]),
                            bcast(POS[:, s, bass.ds(p * 2, 2)].unsqueeze(2), [P, 2, CAP]), ALU.is_equal)
                        if s == 0:
                            ins.then_inc(sel_sig, 1)
                    ins.then_inc(sel_sig, 1)

                def weigh(p, par, wsel_sig):
                    for s in range(S):
                        V.tensor_tensor(
                            WSEL[:, par, s, :].rearrange("p (e c) -> p e c", e=2),
                            SEL[:, par, s, :].rearrange("p (e c) -> p e c", e=2),
                            bcast(CW[:, s, bass.ds(p * 2, 2)].unsqueeze(2), [P, 2, CAP]), ALU.mult)\
                            .then_inc(wsel_sig, 1)

                def select(p, par):
                    build(p, par, sel_ready)
                    dve.wait_ge(sel_ready, p * 2 + (34 * l + 2))
                    weigh(p, par, wsel_ready)

                def xg_half(half, par):
                    return V.tensor_copy(XG[:, par, 4 * half:4 * half + 4, :].rearrange("p k t -> p (k t)"),
                                         PS[:, 4 + half, :])

                def pair(p, par, last=False):
                    t = p + 16 * l
                    dve.wait_ge(silu_ready, t + 1)
                    V.tensor_tensor(ACTB, PS[:, 6, FE:2 * FE], SILB, ALU.mult).then_inc(act_ready, 1)
                    if not last:
                        dve.wait_ge(gather1_done, t + 2)
                        xg_half(1, 1 - par).then_inc(xg1_ready, 1)
                        select(p + 2, par)
                    dve.wait_ge(down0_done, t + 1)
                    V.tensor_copy(YG[:, 0, :], PS[:, 4, :]).then_inc(yg0_ready, 1)

                select(0, 0)
                dve.wait_ge(gather1_done, 16 * l + 1)
                xg_half(1, 0).then_inc(xg1_ready, 1)
                select(1, 1)
                pair(0, 0)
                if l == 0:
                    dve.wait_ge(prep_read, 4)
                    gain_now(2)
                    for s in range(S):
                        V.scalar_tensor_tensor(out=GAIN[:, s, :], in0=GAIN[:, s, :], scalar=1.0, in1=gain[:, :],
                                               op0=ALU.add, op1=ALU.mult).then_inc(scale_ready, 1)
                    dve.wait_ge(scale_ready, 6)
                    V.tensor_copy(small[:, 151:152], small[:, 150:151]).then_inc(gain_used, 1)
                with dve.Fori(0, NPAIR // 2 - 1) as i:
                    pair(i * 2 + 1, 1)
                    pair(i * 2 + 2, 0)
                pair(NPAIR - 1, 1, last=True)
                dve.wait_ge(count_ready, l + 1)
                most = dve.value_load(CNT[0:1, 0:1], min_val=0, max_val=S * P)
                with dve.If(most > CAP):
                    with dve.Fori(0, ROUNDS - 1) as r:
                        V.tensor_scalar(POS[:, :, :], POS[:, :, :], -float(CAP), None, ALU.add).then_inc(ov["shift"], 1)
                        with dve.Fori(0, NPAIR) as p:
                            t = r * NPAIR + p
                            dve.wait_ge(ov["scat"], t + 1)
                            dve.wait_ge(ov["shift"], r + 1)
                            build(p, 0, ov["sel"])
                            dve.wait_ge(ov["sel"], t * 4 + 2)
                            weigh(p, 0, ov["sel"])
                            dve.wait_ge(ov["sil"], t + 1)
                            V.tensor_tensor(ACTB, PS[:, 6, FE:2 * FE], SILB, ALU.mult).then_inc(ov["act"], 1)
                residual(2 * l + 1)

            norm(1)
            evac_ht(1)
            moe(0)
            norm(2)
            evac_ht(2)
            def evac_odd(c):
                bank = 2 * (c % 4)
                dve.wait_ge(used, AT[("odd_in", c)] + 1)
                dst = QKc[:, 1, 512 * c:512 * c + 512] if c < 4 else VY[:, 1, 512 * (c - 4):512 * (c - 4) + 512]
                V.tensor_copy(dst, PS[:, bank + 1, :]).then_inc(odd_free_v, 1)

            xq = QKc[:, 1, :].rearrange("p (n c) -> p n c", n=8)
            c_, s_ = (bcast(cst(x).unsqueeze(1), [P, 4, P]) for x in ("cosc", "sinc"))
            tmp = SF[:, :, :].rearrange("p a (n c) -> p a n c", n=4)

            def rope(part):
                x1, x2 = xq[:, 4 * part:4 * part + 4, 0:P], xq[:, 4 * part:4 * part + 4, P:2 * P]
                st.mark(V.tensor_tensor(tmp[:, 0, :, :], x1, c_, ALU.mult))
                st.mark(V.tensor_tensor(tmp[:, 1, :, :], x2, s_, ALU.mult))
                st.mark(V.tensor_tensor(tmp[:, 2, :, :], x2, c_, ALU.mult))
                st.link(V.tensor_tensor(tmp[:, 3, :, :], x1, s_, ALU.mult))
                st.mark(V.tensor_tensor(x1, tmp[:, 0, :, :], tmp[:, 1, :, :], ALU.subtract))
                st.link(V.tensor_tensor(x2, tmp[:, 2, :, :], tmp[:, 3, :, :], ALU.add))

            evac_odd(0)
            evac_odd(1)
            for h in range(HC):
                dve.wait_ge(powers_ready, 2 * h + 2)
                st.mark(V.tensor_tensor(LGP[:, 0, :], LGP[:, 0, :], cst("ge"), ALU.mult))
                st.link(V.tensor_tensor(LGP[:, 1, :], LGP[:, 1, :], cst("le"), ALU.mult))
                V.tensor_tensor(DM[:, h, :], LGP[:, 0, :], LGP[:, 1, :], ALU.add).then_inc(decay_ready, 1)
            dve.wait_ge(odd_free_v, 2)
            rope(0)
            evac_odd(2)
            evac_odd(3)
            dve.wait_ge(odd_free_a, 4)
            dve.wait_ge(odd_free_v, 4)
            st.link(V.tensor_scalar(QKc[:, 1, 1024:2048], QKc[:, 1, 1024:2048], float(2 * P) ** -0.5, None, ALU.mult))
            V.tensor_scalar(QKc[:, 0, 1024:2048], QKc[:, 0, 1024:2048], float(2 * P) ** -0.5, None, ALU.mult)\
                .then_inc(ret_keys_scaled, 1)
            rope(1)
            V.tensor_copy(small[:, 151:152], small[:, 150:151]).then_inc(ret_rope_done, 1)
            evac_odd(4)

            def gate(i):
                dve.wait_ge(odd_half_read, 6 + i + 1)
                s, h = i // HC, i % HC
                yv = VY[:, s, VC * h:VC * h + VC]
                V.tensor_tensor(yv, yv, GB, ALU.mult).then_inc(gated_ready, 1)

            dve.wait_ge(ret_gain_in, 16)
            dve.wait_ge(decay_ready, HC)
            dve.wait_ge(ret_keys_scaled, 1)
            dve.wait_ge(a_step, ACT_STEPS_KD)
            for s in range(S):
                for h in range(HC):
                    u = HC * s + h
                    if s == 0:
                        if h:
                            dve.wait_ge(ret_state_done, 4 * h)
                        for d in range(2):
                            V.tensor_scalar(KD[:, d, :], QKc[:, 0, 1024 + 256 * h:1024 + 256 * h + 256],
                                            KDC[:, HC * d + h:HC * d + h + 1], None, ALU.mult).then_inc(ret_kd_ready, 1)
                    dve.wait_ge(ret_scores_done, u + 1)
                    if u:
                        dve.wait_ge(ret_out_done, u)
                    V.tensor_tensor(PC, PS[:, 1, 0:P], DM[:, h, :], ALU.mult).then_inc(ret_masked_ready, 1)
                    if s:
                        dve.wait_ge(powers_ready, 2 * HC + 2 * (h + 1))
                        for d in range(2):
                            ins = V.tensor_tensor(QD[:, 2 * d:2 * d + 2, :], TT[:, 0:2, :],
                                                  bcast(LGP[:, d, :].unsqueeze(1), [P, 2, P]), ALU.mult)
                            st.link(ins)
                        V.tensor_copy(small[:, 151:152], small[:, 150:151]).then_inc(ret_qd_ready, 1)
                    if u < 3:
                        c = HEAD_HALVES[u][1][0]
                        dve.wait_ge(used, AT[("odd_in", c)] + 1)
                        V.tensor_copy(VY[:, 1, VC * (c - 4):VC * (c - 3)], PS[:, 3, :]).then_inc(odd_half_read, 1)
                    elif u < 5:
                        gate(2 * u - 6)
                        gate(2 * u - 5)
                    else:
                        gate(u - 1)
                    dve.wait_ge(ret_out_done, u + 1)
                    st.link(V.bn_stats(bnC[:, s, h, :], PS[:, 2, :]))
                    V.bn_aggr(mvC[:, u, :], bnC[:, s, h, :]).then_inc(ret_stats, 1)
                    dve.wait_ge(ret_stats, 2 * u + 2)
                    st.link(V.reciprocal(rsC[:, u:u + 1], sdC[:, u:u + 1]))
                    yv = VY[:, s, VC * h:VC * h + VC]
                    V.tensor_scalar(yv, PS[:, 2, :], mvC[:, u, 0:1], rsC[:, u:u + 1],
                                    ALU.subtract, ALU.mult).then_inc(ret_y_ready, 1)
                    dve.wait_ge(ret_y_ready, u + 1)
                    st.link(V.tensor_tensor(yv, yv, GNC[:, VC * h:VC * h + VC], ALU.mult))
            gate(7)
            dve.wait_ge(gated_turned, 8)
            scaled_gain(3, (4, 6))
            residual(2)
            norm(3)
            evac_ht(3)
            moe(1)
            gain_now(4)
            for s in range(S):
                normalize(4, s, gain[:, :])


ACT_STEPS_KD = 2 + 8 + 8


def shape_constants(np):
    c = np.zeros((P, NCONST), np.float32)

    def put(name, v):
        a, b = CONST_AT[name]
        c[:, a:b] = np.asarray(v, np.float32).reshape(P, b - a)

    t = np.arange(P)
    a, b = t[:, None], t[None, :]
    same = (a // SUB) == (b // SUB)
    put("ident", a == b)
    mid_f, mid_b = (b // SUB) * SUB + SUB // 2 - 1, (b // SUB) * SUB + SUB // 2
    fwd = [1.0 * (same & (a <= b)) - 1.0 * (same & (a <= mid_f)), 1.0 * (same & (a <= b)), 1.0 * (same & (a > b))]
    bwd = [1.0 * (same & (a >= b)) - 1.0 * (same & (a >= mid_b)), 1.0 * (same & (a >= b)), 1.0 * (same & (a < b))]
    put("cums", np.concatenate(fwd + bwd, 1))
    put("relp", np.maximum(b - a, 0))
    put("relm", np.maximum(a - b, 0))
    put("ge", b >= a)
    put("le", b <= a)
    put("powers", np.stack([t + 1, P - t, P - 1 - t, t], 1))
    put("rowf", np.broadcast_to(t + 1, (P, P)))
    put("rowb", np.broadcast_to(P - t, (P, P)))
    row, col = (t // 64).astype(np.float32), (t % 64).astype(np.float32)
    for width, cn, sn in ((128, "cosb", "sinb"), (256, "cosc", "sinc")):
        nf = width // 4
        inv = (10000.0 ** (-np.arange(nf, dtype=np.float64) / nf)).astype(np.float32)
        ang = np.concatenate([row[:, None] * inv, col[:, None] * inv], 1)
        put(cn, np.cos(ang.astype(np.float64)))
        put(sn, np.sin(ang.astype(np.float64)))
    put("upper", a < b)
    put("ones", np.ones((P, P)))
    put("slots", np.broadcast_to(np.arange(CAP), (P, CAP)))
    sel = np.zeros((P, 2, S, 2, P))
    for l in range(2):
        for s in range(S):
            for half in range(2):
                for parity in range(2):
                    sel[32 * (2 * parity + half) + 2 * l + s, l, s, half, :] = 1
    put("selb", sel)
    put("tie4", np.broadcast_to(NG - np.arange(NG), (P, NG)))
    put("tie8", np.broadcast_to(EG - np.arange(EG), (P, EG)))
    return c


_INS = ["x_prompt", "x_sample", "cache_attn_k", "cache_attn_v", "state_hgrn", "state_ret", "c", "c_ctx",
        "mod_w", "mod_b", "norm1_g", "norm2_g", "even_w_in", "even_w_out", "hgrn_lb_logits", "hgrn_norm_g",
        "attn_qn_g", "attn_kn_g", "odd_w_in", "odd_w_out", "ret_decay_logit", "ret_gn_g",
        "moe_w_group", "moe_b_group", "moe_w_expert", "moe_b_expert", "moe_w_gate", "moe_w_up", "moe_w_down",
        "final_norm_g"]
_OUTS = [("y_prompt", (1, P, D)), ("y_sample", (1, P, D)), ("new_attn_k", (1, 1, P, KVH, P)),
         ("new_attn_v", (1, 1, P, KVH, P)), ("new_state_hgrn", (1, 1, 2, HA, P, P)),
         ("new_state_ret", (1, 1, 2, HC, 2 * P, VC))]


def kernel(**inputs):
    import numpy as np
    import concourse.bacc as bacc
    from concourse.bass_utils import run_bass_kernel_spmd as run

    nc = bacc.Bacc("TRN2", target_bir_lowering=False, num_devices=1)
    arrays, ins, outs = {}, {}, {}
    for name in _INS:
        a = np.ascontiguousarray(inputs[name])
        arrays[f"in_{name}"] = a
        ins[name] = nc.dram_tensor(f"in_{name}", a.shape, F32, kind="ExternalInput").ap()
    arrays["in_consts"] = shape_constants(np)
    ins["consts"] = nc.dram_tensor("in_consts", (P, NCONST), F32, kind="ExternalInput").ap()
    for name, shape in _OUTS:
        outs[name] = nc.dram_tensor(f"out_{name}", shape, F32, kind="ExternalOutput").ap()
    backbone(nc, ins, outs)
    r = run(nc, [arrays], core_ids=[0])
    return tuple(r.results[0][f"out_{name}"] for name, _ in _OUTS)
```
